# Optimizing a Trainium2 kernel written in Bass

```python
import math
import jax, jax.numpy as jnp
from jax import lax
import numpy as np

D_MODEL = 1024
BATCH = 1
SEQ = 512
DEPTH = 2
DEC_BATCH = 1
DEC_SEQ = 32
PAST_LEN = 512

CHUNK = 64
BAND_CHUNKS = 8
WINDOW_A = BAND_CHUNKS * CHUNK
HA = 8
DHA = 64
HB = 4
DHB = 64
HC = 4
DHC = 128
N_MEM = 256
REL_CLIP = 128
D_FF = 2816
QBLOCK = 128
D_MIX = HA * DHA + HB * 2 * DHB
D_IN = 3 * HA * DHA + 3 * HB * 2 * DHB
EPS = 1e-6
NEG_INF = -1e30

kernel_name = 'streaming_hybrid_band_diff_encoder'

def rmsnorm(x, g):
    xf = x.astype(jnp.float32)
    y = xf * lax.rsqrt(jnp.mean(xf * xf, axis=-1, keepdims=True) + EPS)
    return (y * g.astype(jnp.float32)).astype(x.dtype)

def swiglu(x, w_gu, w_dn):
    gate, up = jnp.split(x @ w_gu, 2, axis=-1)
    return (jax.nn.silu(gate) * up) @ w_dn

def ffn_half(x, g_pre, g_post, w_gu, w_dn):
    return x + 0.5 * rmsnorm(swiglu(rmsnorm(x, g_pre), w_gu, w_dn), g_post)

def alibi_slopes():
    return jnp.asarray(2.0 ** (-8.0 * np.arange(1, HB + 1) / HB), dtype=jnp.float32)

def rel_bias_lookup(table, rel):
    idx = jnp.clip(rel, -REL_CLIP, REL_CLIP) + REL_CLIP
    return table[:, idx].astype(jnp.float32)

def band_attention_prompt(q, k, v, rel_table):
    B, T = q.shape[:2]
    nc = T // CHUNK
    band = (BAND_CHUNKS + 1) * CHUNK
    qc = q.reshape(B, nc, CHUNK, HA, DHA)
    pad = ((0, 0), (WINDOW_A, 0), (0, 0), (0, 0))
    kp = jnp.pad(k, pad).reshape(B, nc + BAND_CHUNKS, CHUNK, HA, DHA)
    vp = jnp.pad(v, pad).reshape(B, nc + BAND_CHUNKS, CHUNK, HA, DHA)
    kb = jnp.concatenate([kp[:, o:o + nc] for o in range(BAND_CHUNKS + 1)], axis=2)
    vb = jnp.concatenate([vp[:, o:o + nc] for o in range(BAND_CHUNKS + 1)], axis=2)
    i = jnp.arange(CHUNK)
    j = jnp.arange(band)
    bias = rel_bias_lookup(rel_table, i[:, None] - (j[None, :] - WINDOW_A))
    k_pos = (jnp.arange(nc)[:, None] - BAND_CHUNKS) * CHUNK + j[None, :]
    s = jnp.einsum('bcqhd,bckhd->bchqk', qc, kb).astype(jnp.float32) * DHA ** -0.5 + bias
    s = jnp.where((k_pos >= 0)[None, :, None, None, :], s, NEG_INF)
    p = jax.nn.softmax(s, axis=-1)
    o = jnp.einsum('bchqk,bckhd->bcqhd', p.astype(vb.dtype), vb)
    return o.reshape(B, T, HA, DHA)

def band_attention_sample(q, k, v, cache_k, cache_v, past_len, rel_table):
    W = cache_k.shape[1]
    S = q.shape[1]
    k_all = jnp.concatenate([cache_k, k], axis=1)
    v_all = jnp.concatenate([cache_v, v], axis=1)
    q_pos = past_len + jnp.arange(S)
    k_pos = past_len - W + jnp.arange(W + S)
    bias = rel_bias_lookup(rel_table, q_pos[:, None] - k_pos[None, :])
    s = jnp.einsum('bqhd,bkhd->bhqk', q, k_all).astype(jnp.float32) * DHA ** -0.5 + bias
    p = jax.nn.softmax(s, axis=-1)
    return jnp.einsum('bhqk,bkhd->bqhd', p.astype(v_all.dtype), v_all)

def diff_attention(q, k, v, q_pos, k_pos, lam):
    B, Tq = q.shape[:2]
    qb = min(QBLOCK, Tq)
    nb = Tq // qb
    q_blocks = jnp.moveaxis(q.reshape(B, nb, qb, HB, 2, DHB), 1, 0)
    pos_blocks = q_pos.reshape(nb, qb)
    k_chunk = k_pos // CHUNK
    slopes = alibi_slopes()

    def attend_block(args):
        qblk, qp = args
        s = jnp.einsum('bqhid,bkhid->bihqk', qblk, k).astype(jnp.float32) * DHB ** -0.5
        dist = jnp.abs(qp[:, None] - k_pos[None, :]).astype(jnp.float32)
        s = s - slopes[:, None, None] * dist
        visible = k_chunk[None, :] <= (qp // CHUNK)[:, None]
        s = jnp.where(visible, s, NEG_INF)
        p = jax.nn.softmax(s, axis=-1)
        a = p[:, 0] - lam * p[:, 1]
        return jnp.einsum('bhqk,bkhe->bqhe', a.astype(v.dtype), v)

    o = lax.map(attend_block, (q_blocks, pos_blocks))
    return jnp.moveaxis(o, 0, 1).reshape(B, Tq, HB, 2 * DHB)

def cross_attend(q, mem_k, mem_v):
    s = jnp.einsum('bthd,bmhd->bhtm', q, mem_k).astype(jnp.float32) * DHC ** -0.5
    p = jax.nn.softmax(s, axis=-1)
    return jnp.einsum('bhtm,bmhd->bthd', p.astype(mem_v.dtype), mem_v)

def memory_kv(mem, g, w_ckv):
    B = mem.shape[0]
    mk, mv = jnp.split(rmsnorm(mem, g) @ w_ckv, 2, axis=-1)
    return mk.reshape(B, N_MEM, HC, DHC), mv.reshape(B, N_MEM, HC, DHC)

def trunk_layer(l, x, mem_k, mem_v, cache, norm_g, w_ffn_gu, w_ffn_dn, w_in, rel_bias,
                diff_lambda, subln_g, w_out, w_cq, w_co):
    g = norm_g[l]
    x = ffn_half(x, g[0], g[1], w_ffn_gu[l, 0], w_ffn_dn[l, 0])
    u = rmsnorm(x, g[2])
    B, T = u.shape[:2]
    qa, ka, va, qb, kb, vb = jnp.split(u @ w_in[l], 6, axis=-1)
    qa = qa.reshape(B, T, HA, DHA)
    ka = ka.reshape(B, T, HA, DHA)
    va = va.reshape(B, T, HA, DHA)
    qb = qb.reshape(B, T, HB, 2, DHB)
    kb = kb.reshape(B, T, HB, 2, DHB)
    vb = vb.reshape(B, T, HB, 2 * DHB)
    lam_init = 0.8 - 0.6 * math.exp(-0.3 * l)
    lp = diff_lambda[l].astype(jnp.float32)
    lam = jnp.exp(jnp.sum(lp[0] * lp[1])) - jnp.exp(jnp.sum(lp[2] * lp[3])) + lam_init
    if cache is None:
        oa = band_attention_prompt(qa, ka, va, rel_bias[l])
        pos = jnp.arange(T)
        ob = diff_attention(qb, kb, vb, pos, pos, lam)
        keep = min(WINDOW_A, T)
        new_state = (ka[:, T - keep:], va[:, T - keep:], kb, vb)
    else:
        ca_k, ca_v, cb_k, cb_v = cache
        past_len = cb_k.shape[1]
        oa = band_attention_sample(qa, ka, va, ca_k, ca_v, past_len, rel_bias[l])
        kb_all = jnp.concatenate([cb_k, kb], axis=1)
        vb_all = jnp.concatenate([cb_v, vb], axis=1)
        ob = diff_attention(qb, kb_all, vb_all, past_len + jnp.arange(T), jnp.arange(past_len + T), lam)
        new_state = (ka, va, kb, vb)
    ob = rmsnorm(ob, subln_g[l]) * (1.0 - lam_init)
    mix = jnp.concatenate([oa.reshape(B, T, HA * DHA), ob.reshape(B, T, HB * 2 * DHB)], axis=-1) @ w_out[l]
    x = x + rmsnorm(mix, g[3])
    qc = (rmsnorm(x, g[4]) @ w_cq[l]).reshape(B, T, HC, DHC)
    oc = cross_attend(qc, mem_k, mem_v).reshape(B, T, HC * DHC) @ w_co[l]
    x = x + rmsnorm(oc, g[5])
    x = ffn_half(x, g[6], g[7], w_ffn_gu[l, 1], w_ffn_dn[l, 1])
    return x, new_state

def setup_inputs(seed: int = 0) -> dict:
    key = jax.random.key(seed)
    ks = jax.random.split(key, 21)

    def nrm(k, shape, scale):
        return jax.random.normal(k, shape, jnp.float32) * scale

    wa = min(WINDOW_A, PAST_LEN)
    return {
        'x_prompt': nrm(ks[0], (BATCH, SEQ, D_MODEL), 1.0),
        'x_sample': nrm(ks[1], (DEC_BATCH, DEC_SEQ, D_MODEL), 1.0),
        'mem_prompt': nrm(ks[2], (BATCH, N_MEM, D_MODEL), 1.0),
        'cache_a_k': nrm(ks[3], (DEPTH, DEC_BATCH, wa, HA, DHA), 1.0),
        'cache_a_v': nrm(ks[4], (DEPTH, DEC_BATCH, wa, HA, DHA), 1.0),
        'cache_b_k': nrm(ks[5], (DEPTH, DEC_BATCH, PAST_LEN, HB, 2, DHB), 1.0),
        'cache_b_v': nrm(ks[6], (DEPTH, DEC_BATCH, PAST_LEN, HB, 2 * DHB), 1.0),
        'cache_mem_k': nrm(ks[7], (DEPTH, DEC_BATCH, N_MEM, HC, DHC), 1.0),
        'cache_mem_v': nrm(ks[8], (DEPTH, DEC_BATCH, N_MEM, HC, DHC), 1.0),
        'norm_g': 1.0 + nrm(ks[9], (DEPTH, 8, D_MODEL), 0.05),
        'w_ffn_gu': nrm(ks[10], (DEPTH, 2, D_MODEL, 2 * D_FF), D_MODEL ** -0.5),
        'w_ffn_dn': nrm(ks[11], (DEPTH, 2, D_FF, D_MODEL), D_FF ** -0.5),
        'w_in': nrm(ks[12], (DEPTH, D_MODEL, D_IN), D_MODEL ** -0.5),
        'rel_bias': nrm(ks[13], (DEPTH, HA, 2 * REL_CLIP + 1), 0.1),
        'diff_lambda': nrm(ks[14], (DEPTH, 4, DHB), 0.1),
        'subln_g': 1.0 + nrm(ks[15], (DEPTH, 2 * DHB), 0.05),
        'w_out': nrm(ks[16], (DEPTH, D_MIX, D_MODEL), D_MIX ** -0.5),
        'mem_norm_g': 1.0 + nrm(ks[17], (DEPTH, D_MODEL), 0.05),
        'w_cq': nrm(ks[18], (DEPTH, D_MODEL, HC * DHC), D_MODEL ** -0.5),
        'w_ckv': nrm(ks[19], (DEPTH, D_MODEL, 2 * HC * DHC), D_MODEL ** -0.5),
        'w_co': nrm(ks[20], (DEPTH, HC * DHC, D_MODEL), (HC * DHC) ** -0.5),
    }

def reference(x_prompt, x_sample, mem_prompt, cache_a_k, cache_a_v, cache_b_k, cache_b_v,
              cache_mem_k, cache_mem_v, norm_g, w_ffn_gu, w_ffn_dn, w_in, rel_bias, diff_lambda,
              subln_g, w_out, mem_norm_g, w_cq, w_ckv, w_co):
    xp = x_prompt
    xs = x_sample
    p_ak, p_av, p_bk, p_bv, p_mk, p_mv = [], [], [], [], [], []
    s_ak, s_av, s_bk, s_bv = [], [], [], []
    for l in range(DEPTH):
        mk, mv = memory_kv(mem_prompt, mem_norm_g[l], w_ckv[l])
        xp, st_p = trunk_layer(l, xp, mk, mv, None, norm_g, w_ffn_gu, w_ffn_dn, w_in, rel_bias,
                               diff_lambda, subln_g, w_out, w_cq, w_co)
        xs, st_s = trunk_layer(l, xs, cache_mem_k[l], cache_mem_v[l],
                               (cache_a_k[l], cache_a_v[l], cache_b_k[l], cache_b_v[l]),
                               norm_g, w_ffn_gu, w_ffn_dn, w_in, rel_bias,
                               diff_lambda, subln_g, w_out, w_cq, w_co)
        p_ak.append(st_p[0]); p_av.append(st_p[1]); p_bk.append(st_p[2]); p_bv.append(st_p[3])
        p_mk.append(mk); p_mv.append(mv)
        s_ak.append(st_s[0]); s_av.append(st_s[1]); s_bk.append(st_s[2]); s_bv.append(st_s[3])
    return (xp, xs,
            jnp.stack(p_ak), jnp.stack(p_av), jnp.stack(p_bk), jnp.stack(p_bv),
            jnp.stack(p_mk), jnp.stack(p_mv),
            jnp.stack(s_ak), jnp.stack(s_av), jnp.stack(s_bk), jnp.stack(s_bv))


_drawn_inputs = setup_inputs


def setup_inputs(seed=0):
    import zlib

    import numpy as np

    out = dict(_drawn_inputs(seed))
    spreads = {}
    factors = {'rel_bias': 5.054}
    for name, (base, spread) in spreads.items():
        noise = np.random.default_rng([zlib.crc32(name.encode()), seed]).standard_normal(out[name].shape)
        drawn = base * np.exp(spread * noise) if base else spread * noise
        out[name] = __import__('jax').numpy.asarray(drawn.astype(out[name].dtype))
    for name, factor in factors.items():
        out[name] = (out[name] * factor).astype(out[name].dtype)
    return out
```

```python
import math

import numpy as np
import concourse.bass as bass
import concourse.mybir as mybir

F32 = mybir.dt.float32
F32R = mybir.dt.float32r
ACT = mybir.ActivationFunctionType
ALU = mybir.AluOpType
AX = mybir.AxisListType

DEPTH, D, DFF = 2, 1024, 2816
SEQ, SAMPLE, NMEM, PAST = 512, 32, 256, 512
T = SEQ + SAMPLE
H = T // 2
KD = D // 128
KF = DFF // 128
NT = SEQ // 128
TABW = 640
EPS = 1e-6
MASKED = -1e30
SLOPES = [2.0 ** (-8.0 * (h + 1) / 4) for h in range(4)]
LAM_INIT = [0.8 - 0.6 * math.exp(-0.3 * n) for n in range(DEPTH)]

GU, DN, IN, OUT, CKV, CQ, CO = 22, 8, 12, 4, 4, 2, 2
AT_IN = GU + DN
AT_OUT = AT_IN + IN
AT_CKV = AT_OUT + OUT
AT_CQ = AT_CKV + CKV
AT_CO = AT_CQ + CQ
AT_FFN = [0, AT_CO + CO]
PAIRS = AT_FFN[1] + GU + DN
DNB = KF // 2


def rows_of(i):
    return 128 if i < NT else SAMPLE


def keys_of(unit):
    if unit["kind"] == "C":
        return NMEM
    return 128 * (unit["i"] + 1) if unit["i"] < NT else PAST + SAMPLE


def schedule():
    n = {"slot": 0, "score": 0, "unit": 0, "biased": 0, "expd": 0, "turned": 0, "split": 0,
         "cache": 0, "combined": 0}
    slot_users = []

    def use(kind, **more):
        it = {"use": kind, "slot": n["slot"], **more}
        n["slot"] += 1
        slot_users.append(it)
        return it

    def run(units, caches, outs_after):
        steps = []
        for t in range(len(units) + 3):
            uses = []
            for kind, tile in caches.get(t, []):
                uses.append(use("cache", of_kind=kind, tile=tile, cache=n["cache"]))
                n["cache"] += 1
            if t < len(units):
                u = units[t]
                u["unit"] = n["unit"]
                n["unit"] += 1
                u["scores"] = []
                for m in range(2 if u["kind"] == "B" else 1):
                    s = use("score", of=u, map=m, score=n["score"], expd=n["expd"], unit_here=t)
                    n["score"] += 1
                    n["expd"] += 1
                    if u["kind"] != "C":
                        s["biased"] = n["biased"]
                        n["biased"] += 1
                    u["scores"].append(s)
                    uses.append(s)
                if u["kind"] == "B":
                    u["combined"] = n["combined"]
                    n["combined"] += 1
                u["turn_copies"] = 2 if u["i"] == NT and u["kind"] != "C" else 1
                u["turned"] = n["turned"] + u["turn_copies"]
                n["turned"] += u["turn_copies"]
            done = t - 3
            if 0 <= done < len(units) and done in outs_after:
                for tile in outs_after[done]:
                    uses.append(use("out", tile=tile, split=n["split"]))
                    n["split"] += 1
            steps.append({
                "uses": uses,
                "turn": units[t - 1] if 0 <= t - 1 < len(units) else None,
                "value": units[t - 2] if 0 <= t - 2 < len(units) else None,
            })
        return steps

    a = [{"kind": "A", "h": h, "i": i} for h in range(8) for i in range(NT + 1)]
    b = [{"kind": "B", "h": h, "i": i} for h in range(4) for i in range(NT + 1)]
    c = [{"kind": "C", "h": h, "i": i} for h in range(4) for i in range(NT + 1)]
    per = NT + 1
    own = run(a + b, {0: [("A", k) for k in range(4)], len(a): [("B", k) for k in range(4)]},
              {2 * per * p + 2 * per - 1: [p] for p in range(4)} | {len(a + b) - 1: [4, 5, 6, 7]})
    own_count = dict(n)
    cross = run(c, {0: [("C", k) for k in range(2)]}, {per * h + per - 1: [h] for h in range(4)})
    units = a + b + c
    score_owner = [u for u in units for _ in range(2 if u["kind"] == "B" else 1)]
    return own, cross, n, own_count, slot_users, units, score_owner


OWN, CROSS, TOTAL, OWN_COUNT, SLOT_USERS, UNITS, SCORE_OWNER = schedule()


def build(nc, x_prompt, x_sample, mem_prompt, cache_a_k, cache_a_v, cache_b_k, cache_b_v,
          cache_mem_k, cache_mem_v, norm_g, w_ffn_gu, w_ffn_dn, w_in, rel_bias, diff_lambda,
          subln_g, w_out, mem_norm_g, w_cq, w_ckv, w_co, *outs):
    (y_prompt, y_sample, p_a_k, p_a_v, p_b_k, p_b_v, p_mem_k, p_mem_v,
     s_a_k, s_a_v, s_b_k, s_b_v) = outs

    at = [(16512 + 31) // 32 * 32]

    def place(name, shape, dtype=F32, offset=None):
        size = int(np.prod(shape[1:])) * 4
        if offset is None:
            offset = at[0]
            at[0] += (size + 31) // 32 * 32
        return nc.alloc_sbuf_tensor_at(name, shape, dtype, offset=offset)

    x = place("x", [128, KD, T])
    u_hi = place("u_hi", [128, KD, T], F32R)
    u_lo_at = at[0]
    u_lo = place("u_lo", [128, KD, T], F32R)
    y_ffn = place("y_ffn", [128, KD, T], offset=u_lo_at)
    w_raw = place("w_raw", [128, 2, DNB * 128])
    w_hi = place("w_hi", [128, 2, DNB * 128], F32R)
    w_lo = place("w_lo", [128, 2, DNB * 128], F32R)
    square = place("square", [128, 2, T])
    sumsq = place("sumsq", [128, T])
    r_pre = place("r_pre", [128, T])
    root = place("root", [128, T])
    ident = place("ident", [128, 128])
    ones = place("ones", [128, 128])
    eps = place("eps", [128, 1])
    gains_all = place("gains_all", [128, KD, 18])
    gains = place("gains", [128, KD, 10])
    sub_all = place("sub_all", [128, DEPTH])
    neglam_all = place("neglam_all", [128, DEPTH])
    sub_gain = place("sub_gain", [128, 1])
    neglam = place("neglam", [128, 1])
    negmax = place("negmax", [128, 8])
    rowsum = place("rowsum", [128, 8])
    rowinv = place("rowinv", [128, 8])
    mapscale = place("mapscale", [128, 4])
    memsq = place("memsq", [128, 2])
    memroot = place("memroot", [128, 2])
    meminv = place("meminv", [128, 2])
    headsq = place("headsq", [128, 4 * (NT + 1)])
    headroot = place("headroot", [128, 4 * (NT + 1)])
    headinv = place("headinv", [128, 4 * (NT + 1)])
    dist = place("dist", [128, TABW])
    arena = at[0]
    h_hi = place("h_hi", [128, KF, T], F32R)
    h_lo = place("h_lo", [128, KF, T], F32R)
    gate = place("gate", [128, 2, T])
    up = place("up", [128, 2, T])
    at[0] = arena
    qk = place("qk", [128, 16, T])
    v_nat_at = at[0]
    v_nat = place("v_nat", [128, NT + 1, 1024])
    fresh_at = at[0]
    fresh = place("fresh", [128, 2, T])
    kc_t_at = at[0]
    kc_t = place("kc_t", [128, 4, PAST])
    kc_nat_at = at[0]
    kc_nat = place("kc_nat", [128, 2, 512])
    vc_at = at[0]
    vc = place("vc", [128, 4, 512])
    table = place("table", [128, 2, TABW])
    k_nat_at = at[0]
    probs = place("probs", [128, 4, T])
    probs_t = place("probs_t", [128, 2, 640])
    k_nat = place("k_nat", [128, NT + 1, 512], offset=k_nat_at)
    o_nat = place("o_nat", [128, 4, NT + 1, 128])
    y_mix = place("y_mix", [128, KD, T], offset=arena)
    qc = place("qc", [128, 4, T], offset=arena + KD * T * 4)
    mem = place("mem", [128, 2, D], offset=arena + (KD + 4) * T * 4)
    m_hi = place("m_hi", [128, KD, NMEM], F32R, offset=v_nat_at)
    m_lo = place("m_lo", [128, KD, NMEM], F32R, offset=v_nat_at + KD * NMEM * 4)
    mk_t = place("mk_t", [128, 4, NMEM], offset=v_nat_at + 2 * KD * NMEM * 4)
    mv_t = place("mv_t", [128, 2, NMEM], offset=fresh_at)
    cmk_t = place("cmk_t", [128, 4, NMEM], offset=kc_t_at)
    mk_nat = place("mk_nat", [128, 2, 512], offset=kc_t_at + 4 * NMEM * 4)
    cmk_nat = place("cmk_nat", [128, 2, 512], offset=kc_nat_at)
    mv_nat = place("mv_nat", [128, 2, 512], offset=vc_at)
    cmv = place("cmv", [128, 2, 512], offset=vc_at + 4096)
    memsquare = place("memsquare", [128, D], offset=k_nat_at)
    headsquare = place("headsquare", [128, 128], offset=fresh_at)
    x_nat = place("x_nat", [128, NT + 1, D], offset=arena)
    gains_nat = place("gains_nat", [18, D], offset=arena + 24576)
    sub_nat = place("sub_nat", [DEPTH, 128], offset=arena + 28672)
    lam_in = place("lam_in", [128, DEPTH, 4, 64], offset=arena + 29696)
    lam_prod = place("lam_prod", [128, 64], offset=arena + 32768)
    lam_dot = place("lam_dot", [128, 2 * DEPTH], offset=arena + 33280)
    lam_exp = place("lam_exp", [128, 2 * DEPTH], offset=arena + 33536)
    bias_in = place("bias_in", [16, 257], offset=arena + 104448)
    bias_rev = place("bias_rev", [16, 767], offset=arena + 105984)
    masktile = place("masktile", [64, 64], offset=arena + 109568)
    y_nat = place("y_nat", [128, 2, D], offset=arena)

    psum = nc.alloc_psum_tensor("psum", [128, 8, 512], F32)
    flat = psum[:, :, :].rearrange("p b n -> p (b n)")
    rev_dram = nc.dram_tensor("bias_rev_dram", [16, 768], F32, kind="Internal").ap()
    tab_dram = nc.dram_tensor("bias_tab_dram", [16, 128, TABW], F32, kind="Internal").ap()

    def sem(name):
        return nc.alloc_semaphore(name)

    w_loaded = [sem(f"w_loaded{s}") for s in range(2)]
    w_hi_ready, w_lo_ready, chunk_done = sem("w_hi_ready"), sem("w_lo_ready"), sem("chunk_done")
    setup_loaded, x_loaded, consts = sem("setup_loaded"), sem("x_loaded"), sem("consts")
    iden = sem("iden")
    setup_t, setup_done = sem("setup_t"), sem("setup_done")
    rev_ready, rev_stored, tab_made, tab_masked = sem("rev_ready"), sem("rev_stored"), sem("tab_made"), sem("tab_masked")
    lam_dots, lam_exps, dist_ready = sem("lam_dots"), sem("lam_exps"), sem("dist_ready")
    x_turned, x_ready = sem("x_turned"), sem("x_ready")
    layer_gains = sem("layer_gains")
    squared, summed = sem("squared"), sem("summed")
    y_ready = sem("y_ready")
    norm_sum, root_ready, r_ready = sem("norm_sum"), sem("root_ready"), sem("r_ready")
    y_normed = sem("y_normed")
    u_hi_ready, u_lo_ready = sem("u_hi_ready"), sem("u_lo_ready")
    gate_scaled, gate_silu, up_scaled = sem("gate_scaled"), sem("gate_silu"), sem("up_scaled")
    hidden, h_hi_ready, h_lo_ready = sem("hidden"), sem("h_hi_ready"), sem("h_lo_ready")
    fresh_ready, qk_kept, fresh_turned, nat_kept = sem("fresh_ready"), sem("qk_kept"), sem("fresh_turned"), sem("nat_kept")
    k_stored, v_stored = sem("k_stored"), sem("v_stored")
    kc_loaded = [sem(f"kc_loaded{s}") for s in range(2)]
    vc_loaded = sem("vc_loaded")
    tab_loaded = [sem(f"tab_loaded{s}") for s in range(2)]
    tab_scaled = sem("tab_scaled")
    slot_ready, biased, expd, combined = sem("slot_ready"), sem("biased"), sem("expd"), sem("combined")
    split_hi, split_lo, cache_kept = sem("split_hi"), sem("split_lo"), sem("cache_kept")
    rowmax, negated, inverted = sem("rowmax"), sem("negated"), sem("inverted")
    mapscaled = sem("mapscaled")
    turned, turned_kept, values_done, o_kept = sem("turned"), sem("turned_kept"), sem("values_done"), sem("o_kept")
    head_sq, head_root, head_inv, head_normed = sem("head_sq"), sem("head_root"), sem("head_inv"), sem("head_normed")
    mem_loaded, mem_sq, mem_root, mem_inv, mem_normed = [sem("mem_" + n) for n in ("loaded", "sq", "root", "inv", "normed")]
    mem_turned, m_hi_ready, m_lo_ready = sem("mem_turned"), sem("m_hi_ready"), sem("m_lo_ready")
    kv_kept, kv_turned, kv_nat = sem("kv_kept"), sem("kv_turned"), sem("kv_nat")
    cmk_loaded, cmv_loaded, mem_stored = sem("cmk_loaded"), sem("cmv_loaded"), sem("mem_stored")
    qc_ready = sem("qc_ready")
    y_turned, y_kept = sem("y_turned"), sem("y_kept")
    cross_tile, setup_vals, gains_now, rowinverted = sem("cross_tile"), sem("setup_vals"), sem("gains_now"), sem("rowinverted")
    passed = sem("passed")
    y_stored = [sem(f"y_stored{s}") for s in range(2)]

    def two(tile):
        return tile.rearrange("p (b n) -> p b n", b=2)

    def tile_of(tensor, k):
        if isinstance(k, int):
            return tensor[:, k, :]
        return tensor[:, bass.ds(k, 1), :].rearrange("p o n -> p (o n)")

    def banks(b, n=H):
        return psum[:, b:b + 2, 0:n]

    def slot_ap(slot, rows, n, start=0):
        return flat[0:rows, slot * 1024 + start:slot * 1024 + start + n]

    w_gu_v = w_ffn_gu.rearrange("l f (k p) n -> (l f) p k n", p=128)
    w_dn_v = w_ffn_dn.rearrange("l f (k p) n -> (l f) p k n", p=128)
    w_in_v = w_in.rearrange("l (k p) n -> l p k n", p=128)
    w_out_v = w_out.rearrange("l (k p) n -> l p k n", p=128)
    w_ckv_v = w_ckv.rearrange("l (k p) n -> l p k n", p=128)
    w_cq_v = w_cq.rearrange("l (k p) n -> l p k n", p=128)
    w_co_v = w_co.rearrange("l (k p) n -> l p k n", p=128)

    def w_blocks(ring, slot, n=8):
        return ring[:, slot, 0:n * 128]

    def slot_free(index, l):
        it = SLOT_USERS[index]
        if it["use"] == "cache":
            return cache_kept, l * TOTAL["cache"] + it["cache"] + 1
        if it["use"] == "out":
            return split_lo, l * TOTAL["split"] + it["split"] + 1
        if it["of"]["kind"] == "C":
            return expd, l * TOTAL["expd"] + it["expd"] + 1
        return biased, l * TOTAL["biased"] + it["biased"] + 1

    def settled(engine):
        engine.sem_inc(passed)

    block_cm = nc.Block()
    block = block_cm.__enter__()

    @block.sync
    def _(sp):
        def load(pair, slot, src, first=False, n=8):
            if not first:
                sp.wait_ge(w_hi_ready, 2 * pair + slot - 1)
                sp.wait_ge(w_lo_ready, 2 * pair + slot - 1)
            blocks = w_blocks(w_raw, slot, n).rearrange("p (k n) -> p k n", k=src.shape[1])
            sp.dma_start(blocks, src).then_inc(w_loaded[slot], 16)

        def ffn(l, f):
            base = l * PAIRS + AT_FFN[f]
            gu, dn = w_gu_v[2 * l + f], w_dn_v[2 * l + f]
            for s in range(2):
                load(base, s, gu[:, :, s * DFF:s * DFF + 128], first=f == 0)
            with sp.Fori(1, GU) as j:
                for s in range(2):
                    load(base + j, s, gu[:, :, bass.ds(j * 128 + s * DFF, 128)])
            with sp.Fori(0, DN) as m:
                for s in range(2):
                    load(base + GU + m, s, dn[:, s * DNB:(s + 1) * DNB, bass.ds(m * 128, 128)], n=DNB)

        def tiles(base, w, pairs):
            with sp.Fori(0, pairs) as j:
                for s in range(2):
                    load(base + j, s, w[:, :, bass.ds(j * 256 + s * 128, 128)])

        with sp.Fori(0, DEPTH) as l:
            base = l * PAIRS
            sp.wait_ge(x_ready, 32 * l + 1)
            ffn(l, 0)
            tiles(base + AT_IN, w_in_v[l], IN)
            tiles(base + AT_OUT, w_out_v[l], OUT)
            tiles(base + AT_CKV, w_ckv_v[l], CKV)
            tiles(base + AT_CQ, w_cq_v[l], CQ)
            with sp.Fori(0, CO) as j:
                for s in range(2):
                    load(base + AT_CO + j, s, w_co_v[l][:, :, bass.ds(j * 512 + s * 256, 256)])
            ffn(l, 1)

    @block.gpsimd
    def _(pool):
        pool.memset(ident[:, :], 0.0).then_inc(iden, 1)
        pool.memset(ones[:, :], 1.0).then_inc(consts, 1)
        pool.memset(eps[:, :], EPS).then_inc(consts, 1)
        pool.wait_ge(iden, 1)
        pool.affine_select(out=ident[:, :], in_=ident[:, :], compare_op=ALU.not_equal, fill=1.0,
                           base=0, pattern=[[-1, 128]], channel_multiplier=1).then_inc(iden, 1)
        pool.dma_start(gains_nat[0:16, :], norm_g.rearrange("l i d -> (l i) d")).then_inc(setup_loaded, 16)
        pool.dma_start(gains_nat[16:18, :], mem_norm_g).then_inc(setup_loaded, 16)
        pool.dma_start(sub_nat[:, :], subln_g).then_inc(setup_loaded, 16)
        pool.dma_start(lam_in[:, :, :, :].rearrange("p l a d -> p (l a d)"),
                       diff_lambda.rearrange("(o l) a d -> o (l a d)", o=1).broadcast_to([128, DEPTH * 4 * 64])
                       ).then_inc(setup_loaded, 16)
        pool.dma_start(bias_in[:, :], rel_bias.rearrange("l h n -> (l h) n")).then_inc(setup_loaded, 16)
        pool.iota(dist[:, :], [[-1, TABW]], base=PAST, channel_multiplier=1,
                  allow_small_or_imprecise_dtypes=True).then_inc(dist_ready, 1)
        pool.memset(masktile[:, :], MASKED).then_inc(consts, 1)
        pool.wait_ge(rev_ready, 2)
        pool.dma_start(rev_dram[:, 0:767], bias_rev[:, :]).then_inc(rev_stored, 16)
        pool.wait_ge(rev_stored, 16)
        pool.dma_start(tab_dram, bass.AP(rev_dram.tensor, 127, [[768, 16], [-1, 128], [1, TABW]])
                       ).then_inc(tab_made, 16)
        pool.wait_ge(tab_made, 16)
        pool.wait_ge(consts, 3)
        pool.dma_start(tab_dram[:, 0:64, 576:640].rearrange("t p w -> p t w"),
                       masktile[:, :].rearrange("p (t w) -> p t w", t=1).broadcast_to([64, 16, 64])
                       ).then_inc(tab_masked, 16)

        def sum_squares(c):
            for k in range(1, KD):
                pool.wait_ge(squared, 8 * c + k + 1)
                if k == 1:
                    if not isinstance(c, int):
                        pool.wait_ge(norm_sum, c)
                    first = square[:, 0, :]
                else:
                    pool.wait_ge(summed, 7 * c + k - 1)
                    first = sumsq[:, :]
                pool.tensor_tensor(sumsq[:, :], first, square[:, k % 2, :], ALU.add).then_inc(summed, 1)

        def store_keys(l, g, prompt, sample):
            pool.wait_ge(nat_kept, l * 32 + g * 16 + 8)
            settled(pool)
            pool.dma_start(prompt[l].rearrange("(i p) n -> p i n", p=128), k_nat[:, 0:NT, :]).then_inc(k_stored, 16)
            settled(pool)
            pool.dma_start(sample[l], k_nat[0:SAMPLE, NT, :]).then_inc(k_stored, 16)

        def store_values(l, g, prompt, sample):
            pool.wait_ge(nat_kept, l * 32 + g * 16 + 16)
            settled(pool)
            pool.dma_start(prompt[l].rearrange("(i p) n -> p i n", p=128),
                           v_nat[:, 0:NT, g * 512:(g + 1) * 512]).then_inc(v_stored, 16)
            settled(pool)
            pool.dma_start(sample[l], v_nat[0:SAMPLE, NT, g * 512:(g + 1) * 512]).then_inc(v_stored, 16)

        fl = lambda t: t.rearrange("l b t h d -> l (b t) (h d)")
        fl2 = lambda t: t.rearrange("l b t h m d -> l (b t) (h m d)")
        k_outs = [(fl(p_a_k), fl(s_a_k)), (fl2(p_b_k), fl2(s_b_k))]
        v_outs = [(fl(p_a_v), fl(s_a_v)), (fl(p_b_v), fl(s_b_v))]
        k_cache = [fl(cache_a_k), fl2(cache_b_k)]
        v_cache = [fl(cache_a_v), fl(cache_b_v)]

        def load_cache_keys(l, g, k):
            index = g * 4 + k
            if index >= 2:
                pool.wait_ge(slot_ready, l * TOTAL["slot"] + cache_slot[index - 2] + 1)
            settled(pool)
            pool.dma_start(kc_nat[:, k % 2, :], k_cache[g][l][bass.ds(k * 128, 128), :]
                           ).then_inc(kc_loaded[k % 2], 16)

        def load_table(l, h):
            if h >= 2:
                pool.wait_ge(biased, l * TOTAL["biased"] + (h - 1) * (NT + 1))
            settled(pool)
            pool.dma_start(table[:, h % 2, :], tab_dram[l * 8 + h]).then_inc(tab_loaded[h % 2], 16)

        cache_slot = [it["slot"] for it in SLOT_USERS if it["use"] == "cache"]

        sum_squares(0)
        pool.wait_ge(tab_masked, 16)
        with pool.Fori(0, DEPTH) as l:
            sum_squares(8 * l + 1)
            sum_squares(8 * l + 2)
            pool.wait_ge(chunk_done, (l * PAIRS + AT_IN) * 2)
            load_cache_keys(l, 0, 0)
            load_cache_keys(l, 0, 1)
            settled(pool)
            pool.dma_start(vc[:, :, :], v_cache[0][l].rearrange("(k p) n -> p k n", p=128)).then_inc(vc_loaded, 16)
            load_table(l, 0)
            load_table(l, 1)
            store_keys(l, 0, *k_outs[0])
            store_values(l, 0, *v_outs[0])
            store_keys(l, 1, *k_outs[1])
            store_values(l, 1, *v_outs[1])
            load_cache_keys(l, 0, 2)
            load_cache_keys(l, 0, 3)
            load_cache_keys(l, 1, 0)
            load_cache_keys(l, 1, 1)
            for h in range(2, 8):
                load_table(l, h)
            load_cache_keys(l, 1, 2)
            load_cache_keys(l, 1, 3)
            pool.wait_ge(values_done, l * TOTAL["unit"] + 8 * (NT + 1))
            settled(pool)
            pool.dma_start(vc[:, :, :], v_cache[1][l].rearrange("(k p) n -> p k n", p=128)).then_inc(vc_loaded, 16)
            pool.wait_ge(values_done, l * TOTAL["unit"] + 12 * (NT + 1))
            pool.wait_ge(v_stored, l * 64 + 64)
            settled(pool)
            pool.dma_start(mem[:, :, :], mem_prompt.rearrange("b (k p) d -> p (b k) d", p=128)).then_inc(mem_loaded, 16)
            settled(pool)
            pool.dma_start(cmk_nat[:, :, :], fl(cache_mem_k)[l].rearrange("(k p) n -> p k n", p=128)).then_inc(cmk_loaded, 16)
            settled(pool)
            pool.dma_start(cmv[:, :, :], fl(cache_mem_v)[l].rearrange("(k p) n -> p k n", p=128)).then_inc(cmv_loaded, 16)
            sum_squares(8 * l + 3)
            sum_squares(8 * l + 4)
            pool.wait_ge(kv_nat, l * 8 + 4)
            settled(pool)
            pool.dma_start(fl(p_mem_k)[l].rearrange("(k p) n -> p k n", p=128), mk_nat[:, :, :]).then_inc(mem_stored, 16)
            pool.wait_ge(kv_nat, l * 8 + 8)
            settled(pool)
            pool.dma_start(fl(p_mem_v)[l].rearrange("(k p) n -> p k n", p=128), mv_nat[:, :, :]).then_inc(mem_stored, 16)
            sum_squares(8 * l + 5)
            sum_squares(8 * l + 6)
            pool.wait_ge(mem_stored, l * 32 + 32)
            sum_squares(8 * l + 7)
            sum_squares(8 * l + 8)
        pool.wait_ge(k_stored, 64 * DEPTH)
        pool.wait_ge(v_stored, 64 * DEPTH)
        pool.wait_ge(mem_stored, 32 * DEPTH)

    @block.tensor
    def _(pe):
        def turn(out, src):
            rows = src.shape[0]
            return pe.transpose(out, src, ident[0:rows, 0:rows])

        def chunk(pair, slot, bank, inputs, blocks, first, last, count=None):
            pe.wait_ge(w_lo_ready, 2 * pair + slot + 1)
            for b, k in enumerate(blocks):
                if count:
                    count(k)
                product(slot, b, bank, inputs(k), first and b == 0, last and b == len(blocks) - 1)
            return pe_last[0]

        pe_last = [None]

        def product(slot, b, bank, xs, start, stop):
            hi, lo = xs
            wh = w_hi[:, slot, b * 128:(b + 1) * 128]
            wl = w_lo[:, slot, b * 128:(b + 1) * 128]
            n = hi.shape[-1]
            halves = [(0, H), (H, T)] if n == T else [(0, n)]
            for w, xx, s0, s1 in ((wh, hi, start, False), (wh, lo, False, False), (wl, hi, False, stop)):
                for half, (c0, c1) in enumerate(halves):
                    pe_last[0] = pe.matmul(psum[:, bank + half, 0:c1 - c0], w, xx[:, c0:c1], start=s0, stop=s1)

        def norm(c, bank):
            pe.wait_ge(summed, 7 * (c + 1))
            for half in range(2):
                mm = pe.matmul(psum[:, bank + half, 0:H], ones[:, :], sumsq[:, half * H:(half + 1) * H],
                               start=True, stop=True)
            mm.then_inc(norm_sum, 1)

        def u_in(k):
            return u_hi[:, k, :], u_lo[:, k, :]

        def h_in(k):
            return h_hi[:, k, :], h_lo[:, k, :]

        def ffn(l, f):
            q = 4 * l + 3 * f
            n = 2 * l + f
            base = l * PAIRS + AT_FFN[f]

            def tile(pair, bank, local, first=False, head=None):
                for s in range(2):
                    if not first:
                        pe.wait_ge((gate_scaled, up_scaled)[s], n * KF + local - 1)
                    if head and s == 1:
                        head()
                    chunk(pair, s, bank + 2 * s, u_in, range(KD), True, True,
                          count=(lambda k: pe.wait_ge(u_lo_ready, 8 * q + k + 1)) if first and s == 0 and bank == 0 else None
                          ).then_inc(chunk_done, 1)

            tile(base, 0, 0, first=True)
            norm(2 * q, 6)

            def sum_read():
                pe.wait_ge(root_ready, 2 * q + 1)
            tile(base + 1, 4, 1, first=True, head=sum_read)
            with pe.Fori(1, GU // 2) as j:
                tile(base + 2 * j, 0, 2 * j)
                tile(base + 2 * j + 1, 4, 2 * j + 1)
            pe.wait_ge(h_lo_ready, (n + 1) * KF - 1)
            for m in range(2):
                down(q, n, base + GU + m, m, m)
            with pe.Fori(1, DN // 2) as j:
                for m in range(2):
                    down(q, n, base + GU + 2 * j + m, m, 2 * j + m)
            norm(2 * q + 1, 6)

        def down(q, n, pair, parity, m):
            if not (isinstance(m, int) and m < 2):
                pe.wait_ge(y_ready, 8 * q + m - 1)
            chunk(pair, 0, 2 * parity, h_in, range(DNB), True, False).then_inc(chunk_done, 1)
            pe.wait_ge(h_lo_ready, (n + 1) * KF)
            chunk(pair, 1, 2 * parity, h_in, range(DNB, KF), False, True).then_inc(chunk_done, 1)

        def attention(l, steps):
            for step in steps:
                for it in step["uses"]:
                    slot = it["slot"] % 2
                    if it["slot"] >= 2:
                        pe.wait_ge(*slot_free(it["slot"] - 2, l))
                    if it["use"] == "cache":
                        tile, width = it["tile"], 128
                        if it["of_kind"] == "C":
                            pe.wait_ge(cmk_loaded, l * 16 + 16)
                            src = cmk_nat[:, tile, :]
                        else:
                            pe.wait_ge(kc_loaded[tile % 2], l * 64 + 32 * (it["of_kind"] == "B") + 16 * (tile // 2 + 1))
                            src = kc_nat[:, tile % 2, :]
                        for m in range(4):
                            mm = turn(slot_ap(slot, 128, 128, m * 128), src[:, m * 128:(m + 1) * 128])
                    elif it["use"] == "out":
                        if it["tile"] >= 4:
                            pe.wait_ge(head_normed, l * 8 + 2 * (it["tile"] - 3))
                        elif it["slot"] < OWN_COUNT["slot"]:
                            pe.wait_ge(o_kept, l * TOTAL["unit"] + 2 * (NT + 1) * (it["tile"] + 1))
                        else:
                            pe.wait_ge(o_kept, l * TOTAL["unit"] + OWN_COUNT["unit"] + (NT + 1) * (it["tile"] + 1))
                        for i in range(NT + 1):
                            mm = turn(slot_ap(slot, 128, rows_of(i), i * 128),
                                      o_nat[0:rows_of(i), it["tile"] % 4, i, :])
                    else:
                        mm = score(l, it, slot)
                    mm.then_inc(slot_ready, 1)
                u = step["turn"]
                if u:
                    ub, rows = u["unit"] % 2, rows_of(u["i"])
                    if u["kind"] == "B":
                        pe.wait_ge(combined, l * TOTAL["combined"] + u["combined"] + 1)
                    else:
                        pe.wait_ge(expd, l * TOTAL["expd"] + u["scores"][0]["expd"] + 1)
                    if u["unit"] >= 2:
                        pe.wait_ge(turned_kept, l * TOTAL["turned"] + UNITS[u["unit"] - 2]["turned"])
                    settled(pe)
                    p = probs[:, u["scores"][0]["score"] % 4, :]
                    n = keys_of(u)
                    for k in range((n + 127) // 128):
                        keys = min(128, n - k * 128)
                        mm = turn(psum[0:keys, 4 + ub, k * rows:(k + 1) * rows], p[0:rows, k * 128:k * 128 + keys])
                    mm.then_inc(turned, 1)
                u = step["value"]
                if u:
                    ub, rows, h = u["unit"] % 2, rows_of(u["i"]), u["h"]
                    pe.wait_ge(turned_kept, l * TOTAL["turned"] + u["turned"])
                    if u["unit"] >= 2:
                        pe.wait_ge(o_kept, l * TOTAL["unit"] + u["unit"] - 1)
                    n = keys_of(u)
                    if u["i"] == NT:
                        if u["kind"] == "C":
                            pe.wait_ge(cmv_loaded, l * 16 + 16)
                        else:
                            pe.wait_ge(vc_loaded, l * 32 + (16 if u["kind"] == "A" else 32))
                    width = 64 if u["kind"] == "A" else 128
                    tiles = (n + 127) // 128
                    for k in range(tiles):
                        keys = min(128, n - k * 128)
                        at_ = h * width + (512 if u["kind"] == "B" else 0)
                        if u["kind"] == "C":
                            v = (mv_nat if u["i"] < NT else cmv)[:, k, h * 128:(h + 1) * 128]
                        elif u["i"] == NT and k < 4:
                            v = vc[:, k, h * width:(h + 1) * width]
                        else:
                            v = v_nat[0:keys, k, at_:at_ + width]
                        mm = pe.matmul(psum[0:rows, 6 + ub, 0:width],
                                       probs_t[0:keys, ub, k * rows:(k + 1) * rows], v,
                                       start=k == 0, stop=k == tiles - 1)
                    mm.then_inc(values_done, 1)

        def score(l, it, slot):
            u = it["of"]
            h, i = u["h"], u["i"]
            rows, frames = rows_of(i), slice(i * 128, i * 128 + rows_of(i))
            if u["kind"] == "C":
                if i == NT:
                    pe.wait_ge(cache_kept, l * TOTAL["cache"] + TOTAL["cache"])
                keys = (mk_t if i < NT else cmk_t)[:, h, :]
                return pe.matmul(slot_ap(slot, rows, NMEM), qc[:, h, frames], keys, start=True, stop=True)
            if u["kind"] == "A":
                part, tile, base, cached = slice(64 * (h % 2), 64 * (h % 2) + 64), h // 2, 0, 4
            else:
                part, tile, base, cached = slice(64 * it["map"], 64 * it["map"] + 64), h, 8, 8
            q = qk[part, base + tile, frames]
            k = qk[part, base + 4 + tile, :]
            if i < NT:
                return pe.matmul(slot_ap(slot, rows, keys_of(u)), q, k[:, 0:keys_of(u)], start=True, stop=True)
            pe.wait_ge(cache_kept, l * TOTAL["cache"] + cached)
            settled(pe)
            pe.matmul(slot_ap(slot, rows, PAST), q, kc_t[part, tile, :], start=True, stop=True)
            return pe.matmul(slot_ap(slot, rows, SAMPLE, PAST), q, k[:, SEQ:T], start=True, stop=True)

        pe.wait_ge(iden, 2)
        pe.wait_ge(consts, 3)
        pe.wait_ge(setup_loaded, 80)
        for k in range(KD):
            turn(psum[:, 4, k * 18:(k + 1) * 18], gains_nat[:, k * 128:(k + 1) * 128])
        turn(psum[:, 4, KD * 18:KD * 18 + 2], sub_nat[:, :]).then_inc(setup_t, 1)
        pe.wait_ge(x_loaded, 32)
        for k in range(KD):
            if k >= 2:
                pe.wait_ge(x_ready, k - 1)
            for i in range(NT + 1):
                mm = turn(slot_ap(k % 2, 128, rows_of(i), i * 128),
                          x_nat[0:rows_of(i), i, k * 128:(k + 1) * 128])
            mm.then_inc(x_turned, 1)
        pe.wait_ge(x_ready, KD)
        pe.wait_ge(setup_vals, 5)

        with pe.Fori(0, DEPTH) as l:
            base = l * PAIRS
            ffn(l, 0)

            def turn_fresh(g, m):
                index = g * 8 + m - 4
                pe.wait_ge(fresh_ready, l * 24 + g * 12 + m + 1)
                par = m % 2
                if not (isinstance(g, int) and g == 0 and m < 6):
                    pe.wait_ge(nat_kept, l * 32 + 2 * index - 2)
                for i in range(NT + 1):
                    mm = turn(flat[0:rows_of(i), 2048 + par * 1024 + i * 128:2048 + par * 1024 + i * 128 + 128],
                              fresh[:, par, i * 128:i * 128 + rows_of(i)])
                mm.then_inc(fresh_turned, 1)

            q = 4 * l + 1
            for g in range(2):
                for m in range(12):
                    if g or m >= 2:
                        pe.wait_ge(fresh_ready, l * 24 + g * 12 + m - 1)
                    chunk(base + AT_IN + g * 6 + m // 2, m % 2, 2 * (m % 2), u_in, range(KD), True, True,
                          count=(lambda k: pe.wait_ge(u_lo_ready, 8 * q + k + 1)) if g == 0 and m == 0 else None
                          ).then_inc(chunk_done, 1)
                    if g == 0 and m == 0:
                        norm(2 * q, 4)
                    if g == 0 and m == 5:
                        pe.wait_ge(root_ready, 2 * q + 1)
                    if m >= 5:
                        turn_fresh(g, m - 1)
                turn_fresh(g, 11)
            pe.wait_ge(nat_kept, l * 32 + 32)
            pe.wait_ge(qk_kept, l * 16 + 16)
            attention(l, OWN)

            pe.wait_ge(split_lo, l * TOTAL["split"] + OWN_COUNT["split"])
            for m in range(KD):
                if m >= 2:
                    pe.wait_ge(y_ready, 8 * q + m - 1)
                chunk(base + AT_OUT + m // 2, m % 2, 2 * (m % 2), u_in, range(KD), True, True).then_inc(chunk_done, 1)
            norm(2 * q + 1, 6)

            for k in range(KD):
                pe.wait_ge(mem_normed, l * 2 + 2)
                if k >= 2:
                    pe.wait_ge(m_lo_ready, l * 8 + k - 1)
                for i in range(2):
                    mm = turn(psum[:, 4 + k % 2, i * 128:(i + 1) * 128], mem[:, i, k * 128:(k + 1) * 128])
                mm.then_inc(mem_turned, 1)
            pe.wait_ge(y_ready, 8 * (q + 1))
            for m in range(KD + 1):
                if m < KD:
                    if m >= 2:
                        pe.wait_ge(kv_kept, l * 8 + m - 1)
                    chunk(base + AT_CKV + m // 2, m % 2, m % 2, lambda k: (m_hi[:, k, :], m_lo[:, k, :]), range(KD),
                          True, True, count=(lambda k: pe.wait_ge(m_lo_ready, l * 8 + k + 1)) if m == 0 else None
                          ).then_inc(chunk_done, 1)
                if m >= 1:
                    t = m - 1
                    pe.wait_ge(kv_kept, l * 8 + t + 1)
                    if t >= 2:
                        pe.wait_ge(kv_nat, l * 8 + t - 1)
                    src = mk_t[:, t, :] if t < 4 else mv_t[:, t % 2, :]
                    for i in range(2):
                        mm = turn(psum[:, 2 + t % 2, i * 128:(i + 1) * 128], src[:, i * 128:(i + 1) * 128])
                    mm.then_inc(kv_turned, 1)

            q = 4 * l + 2
            for m in range(4):
                if m >= 2:
                    pe.wait_ge(qc_ready, l * 4 + m - 1)
                elif m == 0:
                    pe.wait_ge(kv_nat, l * 8 + 8)
                chunk(base + AT_CQ + m // 2, m % 2, 2 * (m % 2), u_in, range(KD), True, True,
                      count=(lambda k: pe.wait_ge(u_lo_ready, 8 * q + k + 1)) if m == 0 else None).then_inc(chunk_done, 1)
                if m == 0:
                    pe.wait_ge(r_ready, 2 * q)
                    norm(2 * q, 6)
            pe.wait_ge(qc_ready, l * 4 + 4)
            attention(l, CROSS)

            pe.wait_ge(split_lo, (l + 1) * TOTAL["split"])
            for j in range(4):
                pe.wait_ge(w_lo_ready, 2 * (base + AT_CO) + j + 1)
                for t in range(2):
                    m = 2 * j + t
                    if m >= 2:
                        pe.wait_ge(y_ready, 8 * q + m - 1)
                    for k in range(4):
                        product(j % 2, 2 * k + t, 2 * t, u_in(k), k == 0, k == 3)
                    if t == 1:
                        pe_last[0].then_inc(chunk_done, 1)
                    else:
                        pe_last[0].then_inc(cross_tile, 1)
            norm(2 * q + 1, 6)
            ffn(l, 1)

        pe.wait_ge(x_ready, 8 + 64 * DEPTH // 2)
        for i in range(NT + 1):
            if i >= 2:
                pe.wait_ge(y_kept, i - 1)
            for k in range(KD):
                mm = turn(slot_ap(i % 2, rows_of(i), 128, k * 128), x[:, k, i * 128:i * 128 + rows_of(i)])
            mm.then_inc(y_turned, 1)

    @block.scalar
    def _(act):
        def copy(out, src, scale=1.0):
            return act.activation(out, src, ACT.Copy, scale=scale)

        def cut_hi(pair, slot, first=False, n=8):
            act.wait_ge(w_loaded[slot], 16 * (pair + 1))
            if not first:
                act.wait_ge(chunk_done, 2 * pair + slot - 1)
            copy(w_blocks(w_hi, slot, n), w_blocks(w_raw, slot, n)).then_inc(w_hi_ready, 1)

        def square_of(tile, c, k):
            if not (isinstance(c, int) and k < 2):
                act.wait_ge(summed, 7 * c + k - 1)
            act.activation(square[:, k % 2, :], tile, ACT.Square).then_inc(squared, 1)

        def root_of(bank, index, free):
            act.wait_ge(norm_sum, index + 1)
            act.wait_ge(*free)
            act.activation(two(root[:, :]), banks(bank), ACT.Sqrt, bias=eps[:, :], scale=1.0 / D).then_inc(root_ready, 1)

        def keep_y(y, q, m, parity):
            copy(two(tile_of(y, m)), banks(2 * parity)).then_inc(y_ready, 1)
            act.wait_ge(y_ready, 8 * q + m + 1)
            act.wait_ge(summed, 7 * (2 * q + 1) + m - 1)
            act.activation(square[:, parity, :], tile_of(y, m), ACT.Square).then_inc(squared, 1)

        def next_input(q, gain):
            for k in range(KD):
                act.wait_ge(x_ready, 8 * q + k + 1)
                act.activation(u_hi[:, k, :], x[:, k, :], ACT.Copy, scale=gains[:, k, gain:gain + 1]).then_inc(u_hi_ready, 1)
                square_of(x[:, k, :], 2 * q, k)

        def ffn(l, f, next_pairs, gain):
            q, n = 4 * l + 3 * f, 2 * l + f
            base = l * PAIRS + AT_FFN[f]

            def tile(pair, parity, local, n_next=8, head=None):
                cut_hi(pair + 1, 0, n=n_next)
                if head:
                    head()
                act.wait_ge(gate_scaled, n * KF + local + 1)
                act.activation(gate[:, parity, :], gate[:, parity, :], ACT.Silu).then_inc(gate_silu, 1)
                cut_hi(pair + 1, 1, n=n_next)
                act.wait_ge(hidden, n * KF + local + 1)
                copy(tile_of(h_hi, local), up[:, parity, :]).then_inc(h_hi_ready, 1)

            tile(base, 0, 0, head=lambda: root_of(6, 2 * q, (x_ready, 8 * q + 8)))
            tile(base + 1, 1, 1)
            with act.Fori(1, GU // 2 - 1) as j:
                for s in range(2):
                    tile(base + 2 * j + s, s, 2 * j + s)
            tile(base + GU - 2, 0, GU - 2)
            tile(base + GU - 1, 1, GU - 1, n_next=DNB)

            def down(m, parity, cut, n_next):
                cut(m, 0, n_next)
                cut(m, 1, n_next)
                act.wait_ge(chunk_done, 2 * (base + GU + m) + 2)
                keep_y(y_ffn, q, m, parity)

            def cut(m, s, n_next):
                if n_next:
                    cut_hi(base + GU + m + 1, s, n=n_next)
            for m in range(DN - 1):
                down(m, m % 2, cut, DNB)
            down(DN - 1, 1, cut, 8 if next_pairs else 0)
            root_of(6, 2 * q + 1, (r_ready, 2 * q + 1))
            next_input(q + 1, gain)

        def attention(l, steps):
            for step in steps:
                for it in step["uses"]:
                    if it["use"] != "score":
                        continue
                    u = it["of"]
                    rows, n, s = rows_of(u["i"]), keys_of(u), it["score"]
                    p = probs[0:rows, s % 4, 0:n]
                    if u["kind"] == "C":
                        act.wait_ge(negated, l * 20 + it["unit_here"] + 1)
                        if s >= 4:
                            act.wait_ge(turned, l * TOTAL["unit"] + SCORE_OWNER[s - 4]["unit"] + 1)
                        act.activation(p, slot_ap(it["slot"] % 2, rows, n), ACT.Exp, bias=negmax[0:rows, s % 8:s % 8 + 1],
                                       accum_out=rowsum[0:rows, s % 8:s % 8 + 1]).then_inc(expd, 1)
                    else:
                        act.wait_ge(biased, l * TOTAL["biased"] + it["biased"] + 1)
                        act.activation(p, p, ACT.Exp, bias=negmax[0:rows, s % 8:s % 8 + 1], scale=-1.0,
                                       accum_out=rowsum[0:rows, s % 8:s % 8 + 1]).then_inc(expd, 1)
                        if u["kind"] == "B" and u["i"] == 0 and it["map"] == 0 and u["h"] < 3:
                            scale_table(l, u["h"] + 1)
                        if u["kind"] == "A" and u["i"] == 0 and u["h"] == 7:
                            scale_table(l, 0)
                u = step["turn"]
                if u:
                    ub, rows, n = u["unit"] % 2, rows_of(u["i"]), keys_of(u)
                    act.wait_ge(turned, l * TOTAL["unit"] + u["unit"] + 1)
                    if u["unit"] >= 2:
                        act.wait_ge(values_done, l * TOTAL["unit"] + u["unit"] - 1)
                    full = n // 128 * rows
                    copy(probs_t[:, ub, 0:full], psum[:, 4 + ub, 0:full]).then_inc(turned_kept, 1)
                    if n % 128:
                        copy(probs_t[0:n % 128, ub, full:full + rows], psum[0:n % 128, 4 + ub, full:full + rows]
                             ).then_inc(turned_kept, 1)

        def scale_table(l, h):
            act.wait_ge(biased, l * TOTAL["biased"] + (7 * 5 if h == 0 else 40 + 10 * (h - 1)))
            copy(table[:, h % 2, :], dist[:, :], scale=-SLOPES[h]).then_inc(tab_scaled, 1)

        act.dma_start(x_nat[:, 0:NT, :], x_prompt.rearrange("b (i p) d -> p (b i) d", p=128)).then_inc(x_loaded, 16)
        act.dma_start(x_nat[0:SAMPLE, NT, :], x_sample[0]).then_inc(x_loaded, 16)
        act.wait_ge(dist_ready, 1)
        act.activation(dist[:, :], dist[:, :], ACT.Abs).then_inc(dist_ready, 1)
        act.wait_ge(lam_dots, 2 * DEPTH)
        act.activation(lam_exp[:, :], lam_dot[:, :], ACT.Exp).then_inc(lam_exps, 1)
        act.wait_ge(dist_ready, 3)
        act.wait_ge(layer_gains, 1)
        next_input(0, 8)

        with act.Fori(0, DEPTH) as l:
            base = l * PAIRS
            act.wait_ge(x_ready, 32 * l + 1)
            for s in range(2):
                cut_hi(base, s, first=True)
            ffn(l, 0, True, 2)

            q = 4 * l + 1
            for g in range(2):
                for m in range(12):
                    last = g == 1 and m >= 10
                    cut_hi(base + AT_IN + g * 6 + m // 2 + 1, m % 2)
                    if g == 0 and m == 0:
                        root_of(4, 2 * q, (x_ready, 8 * q + 8))
                    if m < 8:
                        act.wait_ge(fresh_ready, l * 24 + g * 12 + m + 1)
                        copy(qk[:, g * 8 + m, :], fresh[:, m % 2, :], scale=0.125 if m < 4 else 1.0).then_inc(qk_kept, 1)
            attention(l, OWN)
            act.wait_ge(head_sq, l * 20 + 20)
            act.activation(headroot[:, :], headsq[:, :], ACT.Sqrt, bias=eps[:, :], scale=1.0 / 128).then_inc(head_root, 1)

            act.wait_ge(mem_loaded, l * 16 + 16)
            act.wait_ge(split_lo, l * TOTAL["split"] + OWN_COUNT["split"])
            for i in range(2):
                if i == 1:
                    act.wait_ge(mem_sq, l * 2 + 1)
                act.activation(memsquare[:, :], mem[:, i, :], ACT.Square, accum_out=memsq[:, i:i + 1]).then_inc(mem_sq, 1)
            act.wait_ge(mem_sq, l * 2 + 2)
            act.activation(memroot[:, :], memsq[:, :], ACT.Sqrt, bias=eps[:, :], scale=1.0 / D).then_inc(mem_root, 1)

            for m in range(KD):
                cut_hi(base + AT_OUT + m // 2 + 1, m % 2)
                act.wait_ge(chunk_done, 2 * (base + AT_OUT) + m + 1)
                keep_y(y_mix, q, m, m % 2)
            root_of(6, 2 * q + 1, (r_ready, 2 * q + 1))
            next_input(q + 1, 4)

            for k in range(KD):
                act.wait_ge(mem_turned, l * 8 + k + 1)
                act.activation(m_hi[:, k, :], psum[:, 4 + k % 2, 0:NMEM], ACT.Copy, scale=gains[:, k, 9:10]).then_inc(m_hi_ready, 1)
            for m in range(KD):
                cut_hi(base + AT_CKV + m // 2 + 1, m % 2)

            q = 4 * l + 2
            for m in range(4):
                cut_hi(base + AT_CQ + m // 2 + 1, m % 2)
                if m == 0:
                    root_of(6, 2 * q, (x_ready, 8 * q + 8))
            attention(l, CROSS)
            for j in range(4):
                cut_hi(base + AT_CO + j // 2 + 1, j % 2)
                for t in range(2):
                    if t == 0:
                        act.wait_ge(cross_tile, l * 4 + j + 1)
                    else:
                        act.wait_ge(chunk_done, 2 * (base + AT_CO) + j + 1)
                    keep_y(y_mix, q, 2 * j + t, t)
            root_of(6, 2 * q + 1, (r_ready, 2 * q + 1))
            next_input(q + 1, 6)
            ffn(l, 1, False, 8)

        for i in range(NT + 1):
            act.wait_ge(y_kept, i + 1)
            dst = y_prompt[0, i * 128:(i + 1) * 128, :] if i < NT else y_sample[0]
            act.dma_start(dst, y_nat[0:rows_of(i), i % 2, :]).then_inc(y_stored[i % 2], 16)
        act.wait_ge(y_stored[0], 48)
        act.wait_ge(y_stored[1], 32)

    @block.vector
    def _(dve):
        def stt(out, a, scalar, b, op0, op1):
            return dve.scalar_tensor_tensor(out=out, in0=a, scalar=scalar, in1=b, op0=op0, op1=op1)

        def cut_lo(pair, slot, n=8):
            dve.wait_ge(w_hi_ready, 2 * pair + slot + 1)
            dve.tensor_tensor(w_blocks(w_lo, slot, n), w_blocks(w_raw, slot, n),
                              w_blocks(w_hi, slot, n).bitcast(F32), ALU.subtract).then_inc(w_lo_ready, 1)

        def inverse(out, index):
            dve.wait_ge(root_ready, index + 1)
            dve.reciprocal(out, root[:, :]).then_inc(r_ready, 1)
            dve.wait_ge(r_ready, index + 1)

        def next_input(q, gain):
            for k in range(KD):
                low_input(q, k, gain)

        def low_input(q, k, gain):
            dve.wait_ge(u_hi_ready, 8 * q + k + 1)
            stt(u_lo[:, k, :], x[:, k, :], gains[:, k, gain:gain + 1], u_hi[:, k, :].bitcast(F32),
                ALU.mult, ALU.subtract).then_inc(u_lo_ready, 1)

        def update(q, y, post, gain):
            inverse(root[:, :], 2 * q + 1)
            for k in range(KD):
                dve.tensor_tensor(y[:, k, :], y[:, k, :], root[:, :], ALU.mult).then_inc(y_normed, 1)
                if k:
                    low_input(q + 1, k - 1, gain)
                dve.wait_ge(y_normed, 8 * q + k + 1)
                stt(x[:, k, :], y[:, k, :], gains[:, k, post:post + 1], x[:, k, :], ALU.mult, ALU.add).then_inc(x_ready, 1)
            low_input(q + 1, KD - 1, gain)

        def ffn(l, f, next_pairs, post, gain):
            q, n = 4 * l + 3 * f, 2 * l + f
            base = l * PAIRS + AT_FFN[f]

            def tile(pair, parity, local, n_next=8, head=None):
                if head:
                    cut_lo(pair + 1, 0, n_next)
                    head()
                dve.wait_ge(chunk_done, 2 * pair + 1)
                if not (isinstance(local, int) and local < 2):
                    dve.wait_ge(h_hi_ready, n * KF + local - 1)
                    dve.wait_ge(h_lo_ready, n * KF + local - 1)
                dve.tensor_tensor(two(gate[:, parity, :]), banks(4 * parity), two(r_pre[:, :]), ALU.mult).then_inc(gate_scaled, 1)
                if not head:
                    cut_lo(pair + 1, 0, n_next)
                dve.wait_ge(chunk_done, 2 * pair + 2)
                dve.tensor_tensor(two(up[:, parity, :]), banks(4 * parity + 2), two(r_pre[:, :]), ALU.mult).then_inc(up_scaled, 1)
                dve.wait_ge(gate_silu, n * KF + local + 1)
                dve.wait_ge(up_scaled, n * KF + local + 1)
                dve.tensor_tensor(up[:, parity, :], up[:, parity, :], gate[:, parity, :], ALU.mult).then_inc(hidden, 1)
                cut_lo(pair + 1, 1, n_next)
                dve.wait_ge(h_hi_ready, n * KF + local + 1)
                dve.tensor_tensor(tile_of(h_lo, local), up[:, parity, :], tile_of(h_hi, local).bitcast(F32),
                                  ALU.subtract).then_inc(h_lo_ready, 1)

            tile(base, 0, 0, head=lambda: inverse(r_pre[:, :], 2 * q))
            tile(base + 1, 1, 1)
            with dve.Fori(1, GU // 2 - 1) as j:
                for s in range(2):
                    tile(base + 2 * j + s, s, 2 * j + s)
            tile(base + GU - 2, 0, GU - 2)
            tile(base + GU - 1, 1, GU - 1, n_next=DNB)
            with dve.Fori(1, DN) as m:
                for s in range(2):
                    cut_lo(base + GU + m, s, DNB)
            if next_pairs:
                for s in range(2):
                    cut_lo(base + GU + DN, s)
            update(q, y_ffn, post, gain)

        def attention(l, steps):
            last = [None]
            for t, step in enumerate(steps):
                u = step["turn"]
                if u and u["kind"] == "B":
                    combine(l, u)
                for it in step["uses"]:
                    slot = it["slot"] % 2
                    if it["use"] == "score":
                        bias(l, it, slot)
                    elif it["use"] == "cache":
                        dve.wait_ge(slot_ready, l * TOTAL["slot"] + it["slot"] + 1)
                        into = (cmk_t if it["of_kind"] == "C" else kc_t)[:, :, it["tile"] * 128:(it["tile"] + 1) * 128]
                        dve.tensor_copy(into, slot_ap(slot, 128, 512).rearrange("p (m n) -> p m n", m=4)).then_inc(cache_kept, 1)
                    elif it["tile"] < 4:
                        out_tile(l, it, slot)
                u = step["value"]
                if u:
                    keep_values(l, u)
            return None

        def out_tile(l, it, slot):
            tile = it["tile"]
            dve.wait_ge(slot_ready, l * TOTAL["slot"] + it["slot"] + 1)
            src = slot_ap(slot, 128, T)
            if tile >= 4:
                dve.tensor_scalar(u_hi[:, tile, :], src, sub_gain[:, :], None, ALU.mult).then_inc(split_hi, 1)
            else:
                dve.tensor_copy(u_hi[:, tile, :], src).then_inc(split_hi, 1)
            dve.wait_ge(split_hi, l * TOTAL["split"] + it["split"] + 1)
            high = u_hi[:, tile, :].bitcast(F32)
            if tile >= 4:
                stt(u_lo[:, tile, :], src, sub_gain[:, :], high, ALU.mult, ALU.subtract).then_inc(split_lo, 1)
            else:
                dve.tensor_tensor(u_lo[:, tile, :], src, high, ALU.subtract).then_inc(split_lo, 1)

        def bias(l, it, slot):
            u, s = it["of"], it["score"]
            rows, n = rows_of(u["i"]), keys_of(u)
            col = slice(s % 8, s % 8 + 1)
            dve.wait_ge(slot_ready, l * TOTAL["slot"] + it["slot"] + 1)
            if u["kind"] == "C":
                dve.reduce_max(negmax[0:rows, col], slot_ap(slot, rows, n), AX.X).then_inc(rowmax, 1)
                dve.wait_ge(rowmax, l * 20 + it["unit_here"] + 1)
                dve.tensor_scalar(negmax[0:rows, col], negmax[0:rows, col], -1.0, None, ALU.mult).then_inc(negated, 1)
                return
            if u["kind"] == "A":
                head = u["h"]
                dve.wait_ge(tab_loaded[head % 2], l * 64 + 16 * (head // 2 + 1))
            else:
                head = u["h"]
                dve.wait_ge(tab_scaled, l * 4 + head + 1)
            if s >= 4:
                dve.wait_ge(turned, l * TOTAL["unit"] + SCORE_OWNER[s - 4]["unit"] + 1)
            settled(dve)
            start = PAST - 128 * u["i"]
            dve.tensor_tensor_reduce(out=probs[0:rows, s % 4, 0:n], in0=slot_ap(slot, rows, n),
                                     in1=table[0:rows, head % 2, start:start + n], scale=-1.0, scalar=3e38,
                                     op0=ALU.add, op1=ALU.min, accum_out=negmax[0:rows, col]).then_inc(biased, 1)

        def combine(l, u):
            s0, s1 = (x_["score"] for x_ in u["scores"])
            rows, n = rows_of(u["i"]), keys_of(u)
            c = l * TOTAL["combined"] + u["combined"]
            par = u["combined"] % 2
            dve.wait_ge(expd, l * TOTAL["expd"] + u["scores"][1]["expd"] + 1)
            dve.reciprocal(rowinv[0:rows, s1 % 8:s1 % 8 + 1], rowsum[0:rows, s1 % 8:s1 % 8 + 1]).then_inc(inverted, 1)
            dve.wait_ge(inverted, c + 1)
            stt(mapscale[0:rows, par:par + 1], rowsum[0:rows, s0 % 8:s0 % 8 + 1], neglam[0:rows, :],
                rowinv[0:rows, s1 % 8:s1 % 8 + 1], ALU.mult, ALU.mult).then_inc(mapscaled, 1)
            dve.wait_ge(mapscaled, c + 1)
            stt(probs[0:rows, s0 % 4, 0:n], probs[0:rows, s1 % 4, 0:n], mapscale[0:rows, par:par + 1],
                probs[0:rows, s0 % 4, 0:n], ALU.mult, ALU.add).then_inc(combined, 1)

        def keep_nat(l, g, m):
            index, par = g * 8 + m - 4, m % 2
            if g == 1 and m == 4:
                dve.wait_ge(k_stored, l * 64 + 32)
            dve.wait_ge(fresh_turned, l * 16 + index + 1)
            into = k_nat[:, :, (m - 4) * 128:(m - 3) * 128] if m < 8 else \
                v_nat[:, :, g * 512 + (m - 8) * 128:g * 512 + (m - 7) * 128]
            src = flat[:, 2048 + par * 1024:2048 + par * 1024 + 640].rearrange("p (i n) -> p i n", n=128)
            dve.tensor_copy(into[:, 0:NT, :], src[:, 0:NT, :]).then_inc(nat_kept, 1)
            dve.tensor_copy(into[0:SAMPLE, NT, :], src[0:SAMPLE, NT, :]).then_inc(nat_kept, 1)

        def keep_values(l, u):
            i, h, s = u["i"], u["h"], u["scores"][0]["score"]
            rows = rows_of(i)
            col = slice(s % 8, s % 8 + 1)
            dve.wait_ge(values_done, l * TOTAL["unit"] + u["unit"] + 1)
            dve.reciprocal(rowinv[0:rows, col], rowsum[0:rows, col]).then_inc(rowinverted, 1)
            dve.wait_ge(rowinverted, l * TOTAL["unit"] + u["unit"] + 1)
            if u["kind"] == "A":
                out, width = o_nat[0:rows, h // 2, i, 64 * (h % 2):64 * (h % 2) + 64], 64
            else:
                out, width = o_nat[0:rows, h, i, :], 128
            dve.tensor_scalar(out, psum[0:rows, 6 + u["unit"] % 2, 0:width], rowinv[0:rows, col], None,
                              ALU.mult).then_inc(o_kept, 1)
            if u["kind"] == "B":
                dve.wait_ge(o_kept, l * TOTAL["unit"] + u["unit"] + 1)
                n = u["combined"]
                if n:
                    dve.wait_ge(head_sq, l * 20 + n)
                dve.tensor_tensor_reduce(out=headsquare[0:rows, :], in0=out, in1=out, scale=1.0, scalar=0.0,
                                         op0=ALU.mult, op1=ALU.add,
                                         accum_out=headsq[0:rows, h * (NT + 1) + i:h * (NT + 1) + i + 1]).then_inc(head_sq, 1)

        dve.memset(headsq[:, :], 1.0).then_inc(setup_done, 1)
        dve.wait_ge(setup_loaded, 80)
        dve.tensor_copy(bias_rev[:, 511:767], bias_in[:, 256:0:-1]).then_inc(rev_ready, 1)
        dve.tensor_copy(bias_rev[:, 0:511], bias_in[:, 256:257].broadcast_to([16, 511])).then_inc(rev_ready, 1)
        for n in range(2 * DEPTH):
            if n:
                dve.wait_ge(lam_dots, n)
            dve.tensor_tensor_reduce(out=lam_prod[:, :], in0=lam_in[:, n // 2, 2 * (n % 2), :],
                                     in1=lam_in[:, n // 2, 2 * (n % 2) + 1, :], scale=1.0, scalar=0.0,
                                     op0=ALU.mult, op1=ALU.add, accum_out=lam_dot[:, n:n + 1]).then_inc(lam_dots, 1)
        dve.wait_ge(dist_ready, 2)
        dve.memset(dist[0:64, 576:640], 1e32).then_inc(dist_ready, 1)
        dve.wait_ge(lam_exps, 1)
        for n in range(DEPTH):
            stt(neglam_all[:, n:n + 1], lam_exp[:, 2 * n + 1:2 * n + 2], LAM_INIT[n],
                lam_exp[:, 2 * n:2 * n + 1], ALU.subtract, ALU.subtract).then_inc(setup_vals, 1)
        dve.wait_ge(setup_t, 1)
        dve.tensor_copy(gains_all[:, :, :], psum[:, 4, 0:KD * 18].rearrange("p (k n) -> p k n", k=KD)).then_inc(setup_vals, 1)
        for n in range(DEPTH):
            dve.tensor_scalar(sub_all[:, n:n + 1], psum[:, 4, KD * 18 + n:KD * 18 + n + 1], 1.0 - LAM_INIT[n], None,
                              ALU.mult).then_inc(setup_vals, 1)
        dve.wait_ge(setup_vals, 5)
        dve.tensor_copy(gains[:, :, 8:9], gains_all[:, :, 0:1]).then_inc(layer_gains, 1)
        dve.wait_ge(layer_gains, 1)
        dve.wait_ge(setup_done, 1)
        for k in range(KD):
            dve.wait_ge(x_turned, k + 1)
            dve.tensor_copy(x[:, k, :], slot_ap(k % 2, 128, T)).then_inc(x_ready, 1)
        for k in range(KD):
            low_input(0, k, 8)

        with dve.Fori(0, DEPTH) as l:
            base = l * PAIRS
            dve.wait_ge(u_lo_ready, 8 + 32 * l)
            dve.tensor_copy(gains[:, :, 0:9], gains_all[:, :, bass.ds(l * 8, 9)]).then_inc(gains_now, 1)
            dve.tensor_copy(gains[:, :, 9:10], gains_all[:, :, bass.ds(l + 16, 1)]).then_inc(gains_now, 1)
            dve.tensor_copy(neglam[:, :], neglam_all[:, bass.ds(l, 1)]).then_inc(gains_now, 1)
            dve.tensor_copy(sub_gain[:, :], sub_all[:, bass.ds(l, 1)]).then_inc(gains_now, 1)
            dve.wait_ge(gains_now, 6 * l + 4)
            for n in (1, 7):
                dve.tensor_scalar(gains[:, :, n:n + 1], gains[:, :, n:n + 1], 0.5, None, ALU.mult).then_inc(gains_now, 1)
            for s in range(2):
                cut_lo(base, s)
            dve.wait_ge(gains_now, 6 * l + 6)
            ffn(l, 0, True, 1, 2)

            q = 4 * l + 1
            for g in range(2):
                for m in range(12):
                    w = g * 12 + m
                    if w == 0:
                        cut_lo(base + AT_IN + 1, 0)
                        inverse(r_pre[:, :], 2 * q)
                    dve.wait_ge(chunk_done, 2 * (base + AT_IN) + w + 1)
                    if w >= 2:
                        before = w - 2
                        bg, bm = divmod(before, 12)
                        if bm < 8:
                            dve.wait_ge(qk_kept, l * 16 + bg * 8 + bm + 1)
                        if bm >= 4:
                            dve.wait_ge(fresh_turned, l * 16 + bg * 8 + bm - 4 + 1)
                    dve.tensor_tensor(two(fresh[:, m % 2, :]), banks(2 * (m % 2)), two(r_pre[:, :]), ALU.mult).then_inc(fresh_ready, 1)
                    if w:
                        cut_lo(base + AT_IN + w // 2 + 1, w % 2)
                    if m >= 5:
                        keep_nat(l, g, m - 1)
                keep_nat(l, g, 11)
            dve.wait_ge(k_stored, l * 64 + 64)
            attention(l, OWN)
            dve.wait_ge(head_root, l + 1)
            dve.reciprocal(headinv[:, :], headroot[:, :]).then_inc(head_inv, 1)
            dve.wait_ge(head_inv, l + 1)
            for h in range(4):
                inv = headinv[:, h * (NT + 1):(h + 1) * (NT + 1)].rearrange("p (i o) -> p i o", o=1)
                o = o_nat[:, h, 0:NT, :]
                dve.tensor_tensor(o, o, inv[:, 0:NT, :].broadcast_to([128, NT, 128]), ALU.mult).then_inc(head_normed, 1)
                o = o_nat[0:SAMPLE, h, NT, :]
                dve.tensor_scalar(o, o, headinv[0:SAMPLE, h * (NT + 1) + NT:(h + 1) * (NT + 1)], None, ALU.mult).then_inc(head_normed, 1)
            for it in OWN[-1]["uses"]:
                out_tile(l, it, it["slot"] % 2)

            dve.wait_ge(mem_root, l + 1)
            dve.reciprocal(meminv[:, :], memroot[:, :]).then_inc(mem_inv, 1)
            dve.wait_ge(mem_inv, l + 1)
            for i in range(2):
                dve.tensor_scalar(mem[:, i, :], mem[:, i, :], meminv[:, i:i + 1], None, ALU.mult).then_inc(mem_normed, 1)

            for m in range(KD):
                cut_lo(base + AT_OUT + m // 2 + 1, m % 2)
            update(q, y_mix, 3, 4)

            for k in range(KD):
                dve.wait_ge(m_hi_ready, l * 8 + k + 1)
                stt(m_lo[:, k, :], psum[:, 4 + k % 2, 0:NMEM], gains[:, k, 9:10], m_hi[:, k, :].bitcast(F32),
                    ALU.mult, ALU.subtract).then_inc(m_lo_ready, 1)
            for m in range(KD + 1):
                if m < KD:
                    dve.wait_ge(chunk_done, 2 * (base + AT_CKV) + m + 1)
                    if m >= 6:
                        dve.wait_ge(kv_turned, l * 8 + m - 1)
                    dst = mk_t[:, m, :] if m < 4 else mv_t[:, m % 2, :]
                    dve.tensor_copy(dst, psum[:, m % 2, 0:NMEM]).then_inc(kv_kept, 1)
                    cut_lo(base + AT_CKV + m // 2 + 1, m % 2)
                if m >= 1:
                    t = m - 1
                    dve.wait_ge(kv_turned, l * 8 + t + 1)
                    dst = (mk_nat if t < 4 else mv_nat)[:, :, (t % 4) * 128:(t % 4 + 1) * 128]
                    dve.tensor_copy(dst, psum[:, 2 + t % 2, 0:NMEM].rearrange("p (i n) -> p i n", i=2)).then_inc(kv_nat, 1)

            q = 4 * l + 2
            for m in range(4):
                cut_lo(base + AT_CQ + m // 2 + 1, m % 2)
                if m == 0:
                    inverse(r_pre[:, :], 2 * q)
                dve.wait_ge(chunk_done, 2 * (base + AT_CQ) + m + 1)
                stt(two(qc[:, m, :]), banks(2 * (m % 2)), 128 ** -0.5, two(r_pre[:, :]), ALU.mult, ALU.mult).then_inc(qc_ready, 1)
            attention(l, CROSS)
            for j in range(4):
                cut_lo(base + AT_CO + j // 2 + 1, j % 2)
            update(q, y_mix, 5, 6)
            dve.wait_ge(mem_stored, l * 32 + 32)
            ffn(l, 1, False, 7, 8)

        for i in range(NT + 1):
            dve.wait_ge(y_turned, i + 1)
            if i >= 2:
                dve.wait_ge(y_stored[i % 2], 16 * (i // 2))
            dve.tensor_copy(y_nat[0:rows_of(i), i % 2, :], slot_ap(i % 2, rows_of(i), D)).then_inc(y_kept, 1)

    block_cm.__exit__(None, None, None)


_INS = ["x_prompt", "x_sample", "mem_prompt", "cache_a_k", "cache_a_v", "cache_b_k", "cache_b_v",
        "cache_mem_k", "cache_mem_v", "norm_g", "w_ffn_gu", "w_ffn_dn", "w_in", "rel_bias",
        "diff_lambda", "subln_g", "w_out", "mem_norm_g", "w_cq", "w_ckv", "w_co"]
_OUTS = [(1, SEQ, D), (1, SAMPLE, D), (DEPTH, 1, SEQ, 8, 64), (DEPTH, 1, SEQ, 8, 64),
         (DEPTH, 1, SEQ, 4, 2, 64), (DEPTH, 1, SEQ, 4, 128), (DEPTH, 1, NMEM, 4, 128), (DEPTH, 1, NMEM, 4, 128),
         (DEPTH, 1, SAMPLE, 8, 64), (DEPTH, 1, SAMPLE, 8, 64), (DEPTH, 1, SAMPLE, 4, 2, 64), (DEPTH, 1, SAMPLE, 4, 128)]


def kernel(**inputs):
    import numpy as _np
    import concourse.bacc as _bacc
    from concourse import mybir as _mybir
    from concourse.bass_utils import run_bass_kernel_spmd as _run

    nc = _bacc.Bacc("TRN2", target_bir_lowering=False, num_devices=1)
    arrays, args = {}, []
    for name in _INS:
        a = _np.ascontiguousarray(inputs[name])
        arrays[f"in_{name}"] = a
        args.append(nc.dram_tensor(f"in_{name}", a.shape, _mybir.dt.from_np(a.dtype), kind="ExternalInput").ap())
    for i, shape in enumerate(_OUTS):
        args.append(nc.dram_tensor(f"out_{i}", shape, _mybir.dt.float32, kind="ExternalOutput").ap())
    build(nc, *args)
    r = _run(nc, [arrays], core_ids=[0])
    return tuple(r.results[0][f"out_{i}"] for i in range(len(_OUTS)))
```

```python
import math

import numpy as np
import concourse.bass as bass
import concourse.mybir as mybir

F32 = mybir.dt.float32
F32R = mybir.dt.float32r
ACT = mybir.ActivationFunctionType
ALU = mybir.AluOpType
AX = mybir.AxisListType

DEPTH, D, DFF = 2, 1024, 2816
SEQ, SAMPLE, NMEM, PAST = 512, 32, 256, 512
T = SEQ + SAMPLE
H = T // 2
KD = D // 128
KF = DFF // 128
NT = SEQ // 128
TABW = 640
EPS = 1e-6
MASKED = -1e30
SLOPES = [2.0 ** (-8.0 * (h + 1) / 4) for h in range(4)]
LAM_INIT = [0.8 - 0.6 * math.exp(-0.3 * n) for n in range(DEPTH)]

GU, DN, IN, OUT, CKV, CQ, CO = 22, 8, 12, 4, 4, 2, 2
AT_IN = GU + DN
AT_OUT = AT_IN + IN
AT_CKV = AT_OUT + OUT
AT_CQ = AT_CKV + CKV
AT_CO = AT_CQ + CQ
AT_FFN = [0, AT_CO + CO]
PAIRS = AT_FFN[1] + GU + DN
DNB = KF // 2


def rows_of(i):
    return 128 if i < NT else SAMPLE


def keys_of(unit):
    if unit["kind"] == "C":
        return NMEM
    return 128 * (unit["i"] + 1) if unit["i"] < NT else PAST + SAMPLE


def schedule():
    n = {"slot": 0, "score": 0, "unit": 0, "biased": 0, "expd": 0, "turned": 0, "split": 0,
         "cache": 0, "combined": 0}
    slot_users = []
    padded = ([], [])
    probs_owner = {}
    n_probs = {"A": 0, "B": 0, "C": 0}

    def use(kind, **more):
        it = {"use": kind, "slot": n["slot"], **more}
        n["slot"] += 1
        slot_users.append(it)
        return it

    def run(units, caches, outs_after):
        turn_at = [t + 2 for t in range(len(units))]
        steps = []
        for t in range(turn_at[-1] + 3):
            uses = []
            for kind, tile in caches.get(t, []):
                uses.append(use("cache", of_kind=kind, tile=tile, cache=n["cache"]))
                n["cache"] += 1
            if t < len(units):
                u = units[t]
                u["unit"] = n["unit"]
                n["unit"] += 1
                u["scores"] = []
                for m in range(2 if u["kind"] == "B" else 1):
                    s = use("score", of=u, map=m, score=n["score"], expd=n["expd"], unit_here=t)
                    n["score"] += 1
                    n["expd"] += 1
                    s["place"] = n_probs[u["kind"]] % (6 if u["kind"] == "B" else 4)
                    n_probs[u["kind"]] += 1
                    s["before"] = probs_owner.get(s["place"])
                    probs_owner[s["place"]] = u
                    if u["kind"] != "C":
                        s["biased"] = n["biased"]
                        n["biased"] += 1
                        side = u["h"] % 2 if u["kind"] == "A" else m
                        s["pad"] = (side, len(padded[side]) % 2)
                        s["pad_free"] = padded[side][-2] if len(padded[side]) >= 2 else None
                        padded[side].append(s["slot"])
                    u["scores"].append(s)
                    uses.append(s)
                if u["kind"] == "B":
                    u["combined"] = n["combined"]
                    n["combined"] += 1
                u["turn_copies"] = 2 if u["i"] == NT and u["kind"] != "C" else 1
                u["turned"] = n["turned"] + u["turn_copies"]
                n["turned"] += u["turn_copies"]
            for last, tiles in outs_after.items():
                if turn_at[last] + 2 == t:
                    for tile in tiles:
                        uses.append(use("out", tile=tile, split=n["split"]))
                        n["split"] += 1
            steps.append({
                "uses": uses,
                "turn": [u for at_, u in zip(turn_at, units) if at_ == t],
                "value": [u for at_, u in zip(turn_at, units) if at_ + 1 == t],
            })
        return steps

    a = [{"kind": "A", "h": h, "i": i} for h in range(8) for i in range(NT + 1)]
    b = [{"kind": "B", "h": h, "i": i} for h in range(4) for i in range(NT + 1)]
    c = [{"kind": "C", "h": h, "i": i} for h in range(4) for i in range(NT + 1)]
    per = NT + 1
    own = run(a + b, {0: [("A", k) for k in range(4)], len(a): [("B", k) for k in range(4)]},
              {2 * per * p + 2 * per - 1: [p] for p in range(4)} | {len(a + b) - 1: [4, 5, 6, 7]})
    own_count = dict(n)
    cross = run(c, {0: [("C", k) for k in range(2)]}, {per * h + per - 1: [h] for h in range(4)})
    return own, cross, n, own_count, slot_users, a + b + c


OWN, CROSS, TOTAL, OWN_COUNT, SLOT_USERS, UNITS = schedule()


def build(nc, x_prompt, x_sample, mem_prompt, cache_a_k, cache_a_v, cache_b_k, cache_b_v,
          cache_mem_k, cache_mem_v, norm_g, w_ffn_gu, w_ffn_dn, w_in, rel_bias, diff_lambda,
          subln_g, w_out, mem_norm_g, w_cq, w_ckv, w_co, *outs):
    (y_prompt, y_sample, p_a_k, p_a_v, p_b_k, p_b_v, p_mem_k, p_mem_v,
     s_a_k, s_a_v, s_b_k, s_b_v) = outs

    at = [(16512 + 31) // 32 * 32]

    def place(name, shape, dtype=F32, offset=None):
        size = int(np.prod(shape[1:])) * 4
        if offset is None:
            offset = at[0]
            at[0] += (size + 31) // 32 * 32
        return nc.alloc_sbuf_tensor_at(name, shape, dtype, offset=offset)

    x = place("x", [128, KD, T])
    u_hi = place("u_hi", [128, KD, T], F32R)
    u_lo_at = at[0]
    u_lo = place("u_lo", [128, KD, T], F32R)
    y_ffn = place("y_ffn", [128, KD, T], offset=u_lo_at)
    w_raw = place("w_raw", [128, 2, DNB * 128])
    w_hi = place("w_hi", [128, 2, DNB * 128], F32R)
    w_lo = place("w_lo", [128, 2, DNB * 128], F32R)
    square = place("square", [128, 2, T])
    sumsq = place("sumsq", [128, T])
    r_pre = place("r_pre", [128, T])
    root = place("root", [128, T])
    root_col = place("root_col", [128, NT + 1])
    inv_col = place("inv_col", [128, NT + 1])
    ident = place("ident", [128, 128])
    ones = place("ones", [128, 128])
    eps = place("eps", [128, 1])
    warmed = place("warmed", [128, 1])
    gains_all = place("gains_all", [128, KD, 18])
    gains = place("gains", [128, KD, 10])
    sub_all = place("sub_all", [128, DEPTH])
    neglam_all = place("neglam_all", [128, DEPTH])
    sub_gain = place("sub_gain", [128, 1])
    neglam = place("neglam", [128, 1])
    headsq = place("headsq", [128, 4 * (NT + 1)])
    masktile_at = at[0]
    negmax = place("negmax", [128, 8])
    rowsum = place("rowsum", [128, 8])
    rowinv = place("rowinv", [128, 8])
    mapscale = place("mapscale", [128, 4])
    memsq = place("memsq", [128, 2])
    memroot = place("memroot", [128, 2])
    meminv = place("meminv", [128, 2])
    headroot = place("headroot", [128, 4 * (NT + 1)])
    headinv = place("headinv", [128, 4 * (NT + 1)])
    q_pad = place("q_pad", [128, 2, 2, 128])
    dist = place("dist", [128, TABW])
    arena = at[0]
    h_hi = place("h_hi", [128, KF, T], F32R)
    h_lo = place("h_lo", [128, KF, T], F32R)
    gate = place("gate", [128, 2, T])
    up = place("up", [128, 2, T])
    at[0] = arena
    qk = place("qk", [128, 16, T])
    v_nat_at = at[0]
    v_nat = place("v_nat", [128, NT + 1, 1024])
    fresh_at = at[0]
    fresh = place("fresh", [128, 2, T])
    kc_t_at = at[0]
    kc_t = place("kc_t", [128, 4, PAST])
    kc_nat_at = at[0]
    kc_nat = place("kc_nat", [128, 2, 512])
    vc_at = at[0]
    vc = place("vc", [128, 4, 512])
    table = place("table", [128, 2, TABW])
    k_nat_at = at[0]
    probs = place("probs", [128, 4, T])
    probs_t = place("probs_t", [128, 2, 512])
    k_nat = place("k_nat", [128, NT + 1, 512], offset=k_nat_at)
    o_nat = place("o_nat", [128, 4, NT + 1, 128])
    y_mix = place("y_mix", [128, KD, T], offset=arena)
    qc = place("qc", [128, 4, T], offset=arena + KD * T * 4)
    mem = place("mem", [128, 2, D], offset=arena + (KD + 4) * T * 4)
    m_hi = place("m_hi", [128, KD, NMEM], F32R, offset=v_nat_at)
    m_lo = place("m_lo", [128, KD, NMEM], F32R, offset=v_nat_at + KD * NMEM * 4)
    mk_t = place("mk_t", [128, 4, NMEM], offset=v_nat_at + 2 * KD * NMEM * 4)
    mv_t = place("mv_t", [128, 2, NMEM], offset=fresh_at)
    cmk_t = place("cmk_t", [128, 4, NMEM], offset=kc_t_at)
    mk_nat = place("mk_nat", [128, 2, 512], offset=kc_t_at + 4 * NMEM * 4)
    cmk_nat = place("cmk_nat", [128, 2, 512], offset=kc_nat_at)
    mv_nat = place("mv_nat", [128, 2, 512], offset=vc_at)
    cmv = place("cmv", [128, 2, 512], offset=vc_at + 4096)
    memsquare = place("memsquare", [128, D], offset=k_nat_at)
    headsquare = place("headsquare", [128, 128], offset=fresh_at)
    x_nat = place("x_nat", [128, NT + 1, D], offset=arena)
    gains_nat = place("gains_nat", [18, D], offset=arena + 24576)
    sub_nat = place("sub_nat", [DEPTH, 128], offset=arena + 28672)
    lam_in = place("lam_in", [128, DEPTH, 4, 64], offset=arena + 29696)
    lam_prod = place("lam_prod", [128, 64], offset=arena + 32768)
    lam_dot = place("lam_dot", [128, 2 * DEPTH], offset=arena + 33280)
    lam_exp = place("lam_exp", [128, 2 * DEPTH], offset=arena + 33536)
    bias_in = place("bias_in", [16, 257], offset=arena + 104448)
    bias_rev = place("bias_rev", [16, 767], offset=arena + 105504)
    masktile = place("masktile", [64, 64], offset=masktile_at)
    y_nat = place("y_nat", [128, 2, D], offset=arena)

    psum = nc.alloc_psum_tensor("psum", [128, 8, 512], F32)
    flat = psum[:, :, :].rearrange("p b n -> p (b n)")
    rev_dram = nc.dram_tensor("bias_rev_dram", [16, 768], F32, kind="Internal").ap()
    tab_dram = nc.dram_tensor("bias_tab_dram", [16, 128, TABW], F32, kind="Internal").ap()

    def sem(name):
        return nc.alloc_semaphore(name)

    w_loaded = [sem(f"w_loaded{s}") for s in range(2)]
    w_hi_ready, w_lo_ready, chunk_done = sem("w_hi_ready"), sem("w_lo_ready"), sem("chunk_done")
    setup_loaded, x_loaded, consts = sem("setup_loaded"), sem("x_loaded"), sem("consts")
    iden = sem("iden")
    setup_t, setup_done = sem("setup_t"), sem("setup_done")
    rev_ready, rev_stored, tab_made, tab_masked = sem("rev_ready"), sem("rev_stored"), sem("tab_made"), sem("tab_masked")
    lam_dots, lam_exps, dist_ready = sem("lam_dots"), sem("lam_exps"), sem("dist_ready")
    x_turned, x_ready = sem("x_turned"), sem("x_ready")
    layer_gains = sem("layer_gains")
    squared, summed = sem("squared"), sem("summed")
    y_ready = sem("y_ready")
    norm_sum, root_ready, r_ready = sem("norm_sum"), sem("root_ready"), sem("r_ready")
    r_spread, r_kept = sem("r_spread"), sem("r_kept")
    y_normed = sem("y_normed")
    u_hi_ready, u_lo_ready = sem("u_hi_ready"), sem("u_lo_ready")
    gate_scaled, gate_silu, up_scaled = sem("gate_scaled"), sem("gate_silu"), sem("up_scaled")
    hidden, h_hi_ready, h_lo_ready = sem("hidden"), sem("h_hi_ready"), sem("h_lo_ready")
    fresh_ready, qk_kept, fresh_turned, nat_kept = sem("fresh_ready"), sem("qk_kept"), sem("fresh_turned"), sem("nat_kept")
    k_stored, v_stored = sem("k_stored"), sem("v_stored")
    kc_loaded = [sem(f"kc_loaded{s}") for s in range(2)]
    vc_loaded = sem("vc_loaded")
    tab_loaded = [sem(f"tab_loaded{s}") for s in range(2)]
    tab_scaled = sem("tab_scaled")
    slot_ready, biased, expd, combined = sem("slot_ready"), sem("biased"), sem("expd"), sem("combined")
    split_hi, split_lo, cache_kept = sem("split_hi"), sem("split_lo"), sem("cache_kept")
    rowmax, negated, inverted = sem("rowmax"), sem("negated"), sem("inverted")
    mapscaled = sem("mapscaled")
    turned, turned_kept, values_done, o_kept = sem("turned"), sem("turned_kept"), sem("values_done"), sem("o_kept")
    head_sq, head_root, head_inv, head_normed = sem("head_sq"), sem("head_root"), sem("head_inv"), sem("head_normed")
    mem_loaded, mem_sq, mem_root, mem_inv, mem_normed = [sem("mem_" + n) for n in ("loaded", "sq", "root", "inv", "normed")]
    mem_turned, m_hi_ready, m_lo_ready = sem("mem_turned"), sem("m_hi_ready"), sem("m_lo_ready")
    kv_kept, kv_turned, kv_nat = sem("kv_kept"), sem("kv_turned"), sem("kv_nat")
    cmk_loaded, cmv_loaded, mem_stored = sem("cmk_loaded"), sem("cmv_loaded"), sem("mem_stored")
    qc_ready = sem("qc_ready")
    y_turned, y_kept = sem("y_turned"), sem("y_kept")
    cross_tile, setup_vals, gains_now, rowinverted = sem("cross_tile"), sem("setup_vals"), sem("gains_now"), sem("rowinverted")
    q_padded = sem("q_padded")
    passed, warm_done = sem("passed"), sem("warm_done")
    y_stored = [sem(f"y_stored{s}") for s in range(2)]

    def two(tile):
        return tile.rearrange("p (b n) -> p b n", b=2)

    def tile_of(tensor, k):
        if isinstance(k, int):
            return tensor[:, k, :]
        return tensor[:, bass.ds(k, 1), :].rearrange("p o n -> p (o n)")

    def banks(b, n=H):
        return psum[:, b:b + 2, 0:n]

    def slot_ap(slot, rows, n, start=0):
        return flat[0:rows, slot * 1024 + start:slot * 1024 + start + n]

    w_gu_v = w_ffn_gu.rearrange("l f (k p) n -> (l f) p k n", p=128)
    w_dn_v = w_ffn_dn.rearrange("l f (k p) n -> (l f) p k n", p=128)
    w_in_v = w_in.rearrange("l (k p) n -> l p k n", p=128)
    w_out_v = w_out.rearrange("l (k p) n -> l p k n", p=128)
    w_ckv_v = w_ckv.rearrange("l (k p) n -> l p k n", p=128)
    w_cq_v = w_cq.rearrange("l (k p) n -> l p k n", p=128)
    w_co_v = w_co.rearrange("l (k p) n -> l p k n", p=128)

    def w_blocks(ring, slot, n=8):
        return ring[:, slot, 0:n * 128]

    def slot_free(index, l):
        it = SLOT_USERS[index]
        if it["use"] == "cache":
            return cache_kept, l * TOTAL["cache"] + it["cache"] + 1
        if it["use"] == "out":
            return split_lo, l * TOTAL["split"] + it["split"] + 1
        if it["of"]["kind"] == "C":
            return expd, l * TOTAL["expd"] + it["expd"] + 1
        return biased, l * TOTAL["biased"] + it["biased"] + 1

    def in_bank(g, m):
        return 6 if (g, m) == (0, 2) else 2 * (m % 2)

    CQ_BANK = (0, 2, 4, 2)

    def probs_at(it):
        return probs[:, it["place"], :] if it["place"] < 4 else square[:, it["place"] - 4, :]

    def settled(engine):
        engine.sem_inc(passed)

    fl = lambda t: t.rearrange("l b t h d -> l (b t) (h d)")
    fl2 = lambda t: t.rearrange("l b t h m d -> l (b t) (h m d)")

    block_cm = nc.Block()
    block = block_cm.__enter__()

    @block.sync
    def _(sp):
        def load(pair, slot, src, first=False, n=8):
            if not first:
                sp.wait_ge(w_hi_ready, 2 * pair + slot - 1)
                sp.wait_ge(w_lo_ready, 2 * pair + slot - 1)
                settled(sp)
            blocks = w_blocks(w_raw, slot, n).rearrange("p (k n) -> p k n", k=src.shape[1])
            sp.dma_start(blocks, src).then_inc(w_loaded[slot], 16)

        def ffn(l, f):
            base = l * PAIRS + AT_FFN[f]
            gu, dn = w_gu_v[2 * l + f], w_dn_v[2 * l + f]
            if f:
                for s in range(2):
                    load(base, s, gu[:, :, s * DFF:s * DFF + 128])
            with sp.Fori(1, GU) as j:
                for s in range(2):
                    load(base + j, s, gu[:, :, bass.ds(j * 128 + s * DFF, 128)])
            with sp.Fori(0, DN) as m:
                for s in range(2):
                    load(base + GU + m, s, dn[:, s * DNB:(s + 1) * DNB, bass.ds(m * 128, 128)], n=DNB)

        def pair(base, w, j):
            for s in range(2):
                load(base + j, s, w[:, :, bass.ds(j * 256 + s * 128, 128)])

        def tiles(base, w, pairs, start=0):
            with sp.Fori(start, pairs) as j:
                pair(base, w, j)

        k_cache = [fl(cache_a_k), fl2(cache_b_k)]
        v_cache = [fl(cache_a_v), fl(cache_b_v)]

        def load_cache_keys(l, g, k):
            index = g * 4 + k
            if index >= 2:
                sp.wait_ge(slot_ready, l * TOTAL["slot"] + cache_slot[index - 2] + 1)
            sp.dma_start(kc_nat[:, k % 2, :], k_cache[g][l][bass.ds(k * 128, 128), :]
                           ).then_inc(kc_loaded[k % 2], 16)

        def load_table(l, h):
            if h >= 2:
                sp.wait_ge(biased, l * TOTAL["biased"] + (h - 1) * (NT + 1))
            sp.dma_start(table[:, h % 2, :], tab_dram[l * 8 + h]).then_inc(tab_loaded[h % 2], 16)

        cache_slot = [it["slot"] for it in SLOT_USERS if it["use"] == "cache"]


        for s in range(2):
            load(0, s, w_gu_v[0][:, :, s * DFF:s * DFF + 128], first=True)
        with sp.Fori(0, DEPTH) as l:
            base = l * PAIRS
            ffn(l, 0)
            pair(base + AT_IN, w_in_v[l], 0)
            pair(base + AT_IN, w_in_v[l], 1)
            sp.wait_ge(chunk_done, (l * PAIRS + AT_IN) * 2)
            load_cache_keys(l, 0, 0)
            load_cache_keys(l, 0, 1)
            sp.dma_start(vc[:, :, :], v_cache[0][l].rearrange("(k p) n -> p k n", p=128)).then_inc(vc_loaded, 16)
            sp.wait_ge(tab_masked, 16)
            load_table(l, 0)
            load_table(l, 1)
            tiles(base + AT_IN, w_in_v[l], IN, 2)
            pair(base + AT_OUT, w_out_v[l], 0)
            pair(base + AT_OUT, w_out_v[l], 1)
            load_cache_keys(l, 0, 2)
            load_cache_keys(l, 0, 3)
            load_cache_keys(l, 1, 0)
            load_cache_keys(l, 1, 1)
            for h in range(2, 8):
                load_table(l, h)
            load_cache_keys(l, 1, 2)
            load_cache_keys(l, 1, 3)
            sp.wait_ge(values_done, l * TOTAL["unit"] + 8 * (NT + 1))
            sp.dma_start(vc[:, :, :], v_cache[1][l].rearrange("(k p) n -> p k n", p=128)).then_inc(vc_loaded, 16)
            sp.wait_ge(values_done, l * TOTAL["unit"] + 12 * (NT + 1))
            sp.wait_ge(v_stored, l * 64 + 64)
            sp.dma_start(mem[:, :, :], mem_prompt.rearrange("b (k p) d -> p (b k) d", p=128)).then_inc(mem_loaded, 16)
            sp.dma_start(cmk_nat[:, :, :], fl(cache_mem_k)[l].rearrange("(k p) n -> p k n", p=128)).then_inc(cmk_loaded, 16)
            sp.dma_start(cmv[:, :, :], fl(cache_mem_v)[l].rearrange("(k p) n -> p k n", p=128)).then_inc(cmv_loaded, 16)
            pair(base + AT_OUT, w_out_v[l], 2)
            pair(base + AT_OUT, w_out_v[l], 3)
            tiles(base + AT_CKV, w_ckv_v[l], CKV)
            tiles(base + AT_CQ, w_cq_v[l], CQ)
            with sp.Fori(0, CO) as j:
                for s in range(2):
                    load(base + AT_CO + j, s, w_co_v[l][:, :, bass.ds(j * 512 + s * 256, 256)])
            ffn(l, 1)
            for s in range(2):
                load(base + PAIRS, s, w_gu_v[(DEPTH - 1 - l) * 2][:, :, s * DFF:s * DFF + 128])

    @block.gpsimd
    def _(pool):
        pool.memset(ident[:, :], 0.0).then_inc(iden, 1)
        pool.memset(ones[:, :], 1.0).then_inc(consts, 1)
        pool.memset(eps[:, :], EPS).then_inc(consts, 1)
        pool.wait_ge(iden, 1)
        pool.affine_select(out=ident[:, :], in_=ident[:, :], compare_op=ALU.not_equal, fill=1.0,
                           base=0, pattern=[[-1, 128]], channel_multiplier=1).then_inc(iden, 1)
        pool.dma_start(gains_nat[0:16, :], norm_g.rearrange("l i d -> (l i) d")).then_inc(setup_loaded, 16)
        pool.dma_start(gains_nat[16:18, :], mem_norm_g).then_inc(setup_loaded, 16)
        pool.dma_start(sub_nat[:, :], subln_g).then_inc(setup_loaded, 16)
        pool.dma_start(lam_in[:, :, :, :].rearrange("p l a d -> p (l a d)"),
                       diff_lambda.rearrange("(o l) a d -> o (l a d)", o=1).broadcast_to([128, DEPTH * 4 * 64])
                       ).then_inc(setup_loaded, 16)
        pool.dma_start(bias_in[:, :], rel_bias.rearrange("l h n -> (l h) n")).then_inc(setup_loaded, 16)
        pool.iota(dist[:, :], [[-1, TABW]], base=PAST, channel_multiplier=1,
                  allow_small_or_imprecise_dtypes=True).then_inc(dist_ready, 1)
        pool.memset(q_pad[:, :, :, :], 0.0).then_inc(consts, 1)
        pool.memset(masktile[:, :], MASKED).then_inc(consts, 1)
        pool.wait_ge(rev_ready, 2)
        pool.dma_start(rev_dram[:, 0:767], bias_rev[:, :]).then_inc(rev_stored, 16)
        pool.wait_ge(rev_stored, 16)
        pool.dma_start(tab_dram, bass.AP(rev_dram.tensor, 127, [[768, 16], [-1, 128], [1, TABW]])
                       ).then_inc(tab_made, 16)
        pool.wait_ge(tab_made, 16)
        pool.wait_ge(consts, 4)
        pool.dma_start(tab_dram[:, 0:64, 576:640].rearrange("t p w -> p t w"),
                       masktile[:, :].rearrange("p (t w) -> p t w", t=1).broadcast_to([64, 16, 64])
                       ).then_inc(tab_masked, 16)

        def sum_x_squares(q):
            for k in range(1, KD):
                pool.wait_ge(squared, 16 * q + k + 1)
                if k == 1:
                    if not isinstance(q, int):
                        pool.wait_ge(norm_sum, 2 * q)
                    first = square[:, 0, :]
                else:
                    pool.wait_ge(summed, 14 * q + k - 1)
                    first = sumsq[:, :]
                pool.tensor_tensor(sumsq[:, :], first, square[:, k % 2, :], ALU.add).then_inc(summed, 1)

        def store_keys(l, g, prompt, sample):
            pool.wait_ge(nat_kept, l * 32 + g * 16 + 8)
            settled(pool)
            pool.dma_start(prompt[l].rearrange("(i p) n -> p i n", p=128), k_nat[:, 0:NT, :]).then_inc(k_stored, 16)
            settled(pool)
            pool.dma_start(sample[l], k_nat[0:SAMPLE, NT, :]).then_inc(k_stored, 16)

        def store_values(l, g, prompt, sample):
            pool.wait_ge(nat_kept, l * 32 + g * 16 + 16)
            settled(pool)
            pool.dma_start(prompt[l].rearrange("(i p) n -> p i n", p=128),
                           v_nat[:, 0:NT, g * 512:(g + 1) * 512]).then_inc(v_stored, 16)
            settled(pool)
            pool.dma_start(sample[l], v_nat[0:SAMPLE, NT, g * 512:(g + 1) * 512]).then_inc(v_stored, 16)

        def pad_query(l, it):
            u, (side, place_) = it["of"], it["pad"]
            part = slice(64 * side, 64 * side + 64)
            tile = u["h"] // 2 if u["kind"] == "A" else 8 + u["h"]
            rows = rows_of(u["i"])
            if it["pad_free"] is not None:
                pool.wait_ge(slot_ready, l * TOTAL["slot"] + it["pad_free"] + 1)
                settled(pool)
            pool.tensor_copy(q_pad[part, side, place_, 0:rows], qk[part, tile, u["i"] * 128:u["i"] * 128 + rows]
                             ).then_inc(q_padded, 1)

        k_outs = [(fl(p_a_k), fl(s_a_k)), (fl2(p_b_k), fl2(s_b_k))]
        v_outs = [(fl(p_a_v), fl(s_a_v)), (fl(p_b_v), fl(s_b_v))]
        sum_x_squares(0)
        with pool.Fori(0, DEPTH) as l:
            sum_x_squares(4 * l + 1)
            store_keys(l, 0, *k_outs[0])
            store_values(l, 0, *v_outs[0])
            store_keys(l, 1, *k_outs[1])
            pool.wait_ge(qk_kept, l * 16 + 16)
            settled(pool)
            for it in SLOT_USERS:
                if "pad" in it:
                    pad_query(l, it)
                    if it["biased"] == 5:
                        store_values(l, 1, *v_outs[1])
            sum_x_squares(4 * l + 2)
            pool.wait_ge(kv_nat, l * 8 + 4)
            settled(pool)
            pool.dma_start(fl(p_mem_k)[l].rearrange("(k p) n -> p k n", p=128), mk_nat[:, :, :]).then_inc(mem_stored, 16)
            pool.wait_ge(kv_nat, l * 8 + 8)
            settled(pool)
            pool.dma_start(fl(p_mem_v)[l].rearrange("(k p) n -> p k n", p=128), mv_nat[:, :, :]).then_inc(mem_stored, 16)
            sum_x_squares(4 * l + 3)
            pool.wait_ge(mem_stored, l * 32 + 32)
            sum_x_squares(4 * l + 4)
        pool.wait_ge(k_stored, 64 * DEPTH)
        pool.wait_ge(v_stored, 64 * DEPTH)
        pool.wait_ge(mem_stored, 32 * DEPTH)

    @block.tensor
    def _(pe):
        def turn(out, src):
            rows = src.shape[0]
            return pe.transpose(out, src, ident[0:rows, 0:rows])

        def chunk(pair, slot, bank, inputs, blocks, first, last, count=None):
            pe.wait_ge(w_lo_ready, 2 * pair + slot + 1)
            for b, k in enumerate(blocks):
                if count:
                    count(k)
                product(slot, b, bank, inputs(k), first and b == 0, last and b == len(blocks) - 1)
            return pe_last[0]

        pe_last = [None]

        def product(slot, b, bank, xs, start, stop):
            hi, lo = xs
            wh = w_hi[:, slot, b * 128:(b + 1) * 128]
            wl = w_lo[:, slot, b * 128:(b + 1) * 128]
            n = hi.shape[-1]
            halves = [(0, H), (H, T)] if n == T else [(0, n)]
            for w, xx, s0, s1 in ((wh, hi, start, False), (wh, lo, False, False), (wl, hi, False, stop)):
                for half, (c0, c1) in enumerate(halves):
                    pe_last[0] = pe.matmul(psum[:, bank + half, 0:c1 - c0], w, xx[:, c0:c1], start=s0, stop=s1)

        def norm_x(q, bank):
            pe.wait_ge(summed, 14 * q + 7)
            for half in range(2):
                mm = pe.matmul(psum[:, bank + half, 0:H], ones[:, :], sumsq[:, half * H:(half + 1) * H],
                               start=True, stop=True)
            mm.then_inc(norm_sum, 1)

        def norm_y(q):
            pe.wait_ge(summed, 14 * q + 14)
            for i in range(NT + 1):
                start = min(i * 128, T - 128)
                mm = pe.matmul(psum[:, 6, i:i + 1], sumsq[:, start:start + 128], ones[:, 0:1], start=True, stop=True)
            mm.then_inc(norm_sum, 1)

        def spread_r(q):
            pe.wait_ge(r_ready, 2 * q + 2)
            for i in range(NT):
                turn(flat[:, 3072 + i * 128:3072 + i * 128 + 128], inv_col[:, i:i + 1].broadcast_to([128, 128]))
            pe.matmul(flat[:, 3072 + SEQ:3072 + T], inv_col[:, NT:NT + 1].broadcast_to([128, 128]),
                      ident[:, 128 - SAMPLE:128], start=True, stop=True).then_inc(r_spread, 1)

        def first_chunks(pair, q):
            pe.wait_ge(w_lo_ready, 2 * pair + 2)
            for k in range(KD):
                pe.wait_ge(u_lo_ready, 8 * q + k + 1)
                for s in range(2):
                    product(s, k, 2 * s, u_in(k), k == 0, k == KD - 1)
                    if k == KD - 1:
                        pe_last[0].then_inc(chunk_done, 1)

        def u_in(k):
            return u_hi[:, k, :], u_lo[:, k, :]

        def h_in(k):
            return h_hi[:, k, :], h_lo[:, k, :]

        def ffn(l, f):
            q = 4 * l + 3 * f
            n = 2 * l + f
            base = l * PAIRS + AT_FFN[f]

            def tile(pair, bank, local, first=False, head=None):
                for s in range(2):
                    if not first:
                        pe.wait_ge((gate_scaled, up_scaled)[s], n * KF + local - 1)
                    if head and s == 1:
                        head()
                    chunk(pair, s, bank + 2 * s, u_in, range(KD), True, True).then_inc(chunk_done, 1)

            first_chunks(base, q)
            norm_x(q, 6)

            def sum_read():
                pe.wait_ge(root_ready, 2 * q + 1)
            tile(base + 1, 4, 1, first=True, head=sum_read)
            with pe.Fori(1, GU // 2) as j:
                tile(base + 2 * j, 0, 2 * j)
                tile(base + 2 * j + 1, 4, 2 * j + 1)
            pe.wait_ge(h_lo_ready, (n + 1) * KF - 1)
            for m in range(2):
                down(q, n, base + GU + m, m, m)
            with pe.Fori(1, DN // 2) as j:
                for m in range(2):
                    down(q, n, base + GU + 2 * j + m, m, 2 * j + m)
            norm_y(q)
            spread_r(q)

        def down(q, n, pair, parity, m):
            if not (isinstance(m, int) and m < 2):
                pe.wait_ge(y_ready, 8 * q + m - 1)
            chunk(pair, 0, 2 * parity, h_in, range(DNB), True, False).then_inc(chunk_done, 1)
            pe.wait_ge(h_lo_ready, (n + 1) * KF)
            chunk(pair, 1, 2 * parity, h_in, range(DNB, KF), False, True).then_inc(chunk_done, 1)

        def attention(l, steps):
            for step in steps:
                for it in step["uses"]:
                    slot = it["slot"] % 2
                    if it["slot"] >= 2:
                        pe.wait_ge(*slot_free(it["slot"] - 2, l))
                    if it["use"] == "cache":
                        tile, width = it["tile"], 128
                        if it["of_kind"] == "C":
                            pe.wait_ge(cmk_loaded, l * 16 + 16)
                            src = cmk_nat[:, tile, :]
                        else:
                            pe.wait_ge(kc_loaded[tile % 2], l * 64 + 32 * (it["of_kind"] == "B") + 16 * (tile // 2 + 1))
                            src = kc_nat[:, tile % 2, :]
                        for m in range(4):
                            mm = turn(slot_ap(slot, 128, 128, m * 128), src[:, m * 128:(m + 1) * 128])
                    elif it["use"] == "out":
                        if it["tile"] >= 4:
                            pe.wait_ge(head_normed, l * 8 + 2 * (it["tile"] - 3))
                        elif it["slot"] < OWN_COUNT["slot"]:
                            pe.wait_ge(o_kept, l * TOTAL["unit"] + 2 * (NT + 1) * (it["tile"] + 1))
                        else:
                            pe.wait_ge(o_kept, l * TOTAL["unit"] + OWN_COUNT["unit"] + (NT + 1) * (it["tile"] + 1))
                        for i in range(NT + 1):
                            mm = turn(slot_ap(slot, 128, rows_of(i), i * 128),
                                      o_nat[0:rows_of(i), it["tile"] % 4, i, :])
                    else:
                        mm = score(l, it, slot)
                    mm.then_inc(slot_ready, 1)
                for u in step["turn"]:
                    ub, rows = u["unit"] % 2, rows_of(u["i"])
                    if u["kind"] == "B":
                        pe.wait_ge(combined, l * TOTAL["combined"] + u["combined"] + 1)
                    else:
                        pe.wait_ge(expd, l * TOTAL["expd"] + u["scores"][0]["expd"] + 1)
                    if u["unit"] == 0:
                        pe.wait_ge(nat_kept, l * 32 + 32)
                    if u["unit"] >= 2:
                        pe.wait_ge(turned_kept, l * TOTAL["turned"] + UNITS[u["unit"] - 2]["turned"])
                    settled(pe)
                    p = probs_at(u["scores"][0])
                    n = keys_of(u)
                    for k in range((n + 127) // 128):
                        keys = min(128, n - k * 128)
                        mm = turn(psum[0:keys, 4 + ub, k * rows:(k + 1) * rows], p[0:rows, k * 128:k * 128 + keys])
                    mm.then_inc(turned, 1)
                for u in step["value"]:
                    ub, rows, h = u["unit"] % 2, rows_of(u["i"]), u["h"]
                    pe.wait_ge(turned_kept, l * TOTAL["turned"] + u["turned"])
                    if u["unit"] >= 2:
                        pe.wait_ge(o_kept, l * TOTAL["unit"] + u["unit"] - 1)
                    n = keys_of(u)
                    if u["i"] == NT:
                        if u["kind"] == "C":
                            pe.wait_ge(cmv_loaded, l * 16 + 16)
                        else:
                            pe.wait_ge(vc_loaded, l * 32 + (16 if u["kind"] == "A" else 32))
                    tiles = (n + 127) // 128
                    tile = h // 2 if u["kind"] == "A" else h
                    for k in range(tiles):
                        keys = min(128, n - k * 128)
                        at_ = tile * 128 + (512 if u["kind"] == "B" else 0)
                        if u["kind"] == "C":
                            v = (mv_nat if u["i"] < NT else cmv)[:, k, h * 128:(h + 1) * 128]
                        elif u["i"] == NT and k < 4:
                            v = vc[:, k, tile * 128:(tile + 1) * 128]
                        else:
                            v = v_nat[0:keys, k, at_:at_ + 128]
                        mm = pe.matmul(psum[0:rows, 6 + ub, 0:128],
                                       probs_t[0:keys, ub, k * rows:(k + 1) * rows], v,
                                       start=k == 0, stop=k == tiles - 1)
                    mm.then_inc(values_done, 1)

        def score(l, it, slot):
            u = it["of"]
            h, i = u["h"], u["i"]
            rows, frames = rows_of(i), slice(i * 128, i * 128 + rows_of(i))
            if u["kind"] == "C":
                if i == NT:
                    pe.wait_ge(cache_kept, l * TOTAL["cache"] + TOTAL["cache"])
                keys = (mk_t if i < NT else cmk_t)[:, h, :]
                return pe.matmul(slot_ap(slot, rows, NMEM), qc[:, h, frames], keys, start=True, stop=True)
            tile, base, cached = (h // 2, 0, 4) if u["kind"] == "A" else (h, 8, 8)
            pe.wait_ge(q_padded, l * TOTAL["biased"] + it["biased"] + 1)
            q = q_pad[:, it["pad"][0], it["pad"][1], 0:rows]
            k = qk[:, base + 4 + tile, :]
            if i < NT:
                return pe.matmul(slot_ap(slot, rows, keys_of(u)), q, k[:, 0:keys_of(u)], start=True, stop=True)
            pe.wait_ge(cache_kept, l * TOTAL["cache"] + cached)
            pe.matmul(slot_ap(slot, rows, PAST), q, kc_t[:, tile, :], start=True, stop=True)
            return pe.matmul(slot_ap(slot, rows, SAMPLE, PAST), q, k[:, SEQ:T], start=True, stop=True)

        pe.wait_ge(iden, 2)
        pe.wait_ge(consts, 4)
        pe.wait_ge(setup_loaded, 80)
        for k in range(KD):
            turn(psum[:, 4, k * 18:(k + 1) * 18], gains_nat[:, k * 128:(k + 1) * 128])
        turn(psum[:, 4, KD * 18:KD * 18 + 2], sub_nat[:, :]).then_inc(setup_t, 1)
        pe.wait_ge(x_loaded, 32)
        for k in range(KD):
            if k >= 2:
                pe.wait_ge(x_ready, k - 1)
            for i in range(NT + 1):
                mm = turn(slot_ap(k % 2, 128, rows_of(i), i * 128),
                          x_nat[0:rows_of(i), i, k * 128:(k + 1) * 128])
            mm.then_inc(x_turned, 1)
        pe.wait_ge(x_ready, KD)
        pe.wait_ge(setup_vals, 5)

        with pe.Fori(0, DEPTH) as l:
            base = l * PAIRS
            ffn(l, 0)

            def turn_fresh(g, m):
                index = g * 8 + m - 4
                pe.wait_ge(fresh_ready, l * 24 + g * 12 + m + 1)
                par = m % 2
                if not (isinstance(g, int) and g == 0 and m < 6):
                    pe.wait_ge(nat_kept, l * 32 + 2 * index - 2)
                for i in range(NT + 1):
                    mm = turn(flat[0:rows_of(i), 2048 + par * 1024 + i * 128:2048 + par * 1024 + i * 128 + 128],
                              fresh[:, par, i * 128:i * 128 + rows_of(i)])
                mm.then_inc(fresh_turned, 1)

            q = 4 * l + 1
            for g in range(2):
                for m in range(12):
                    if g or m >= 3:
                        pe.wait_ge(fresh_ready, l * 24 + g * 12 + m - 1)
                    if g == 0 and m == 0:
                        first_chunks(base + AT_IN, q)
                        norm_x(q, 4)
                    elif g or m >= 2:
                        chunk(base + AT_IN + g * 6 + m // 2, m % 2, in_bank(g, m), u_in, range(KD), True, True
                              ).then_inc(chunk_done, 1)
                    if g == 0 and m == 5:
                        pe.wait_ge(root_ready, 2 * q + 1)
                    if m >= 5:
                        turn_fresh(g, m - 1)
                turn_fresh(g, 11)
            pe.wait_ge(fresh_ready, l * 24 + 24)
            pe.wait_ge(qk_kept, l * 16 + 16)
            attention(l, OWN)

            pe.wait_ge(split_lo, l * TOTAL["split"] + OWN_COUNT["split"])
            for m in range(KD):
                if m >= 2:
                    pe.wait_ge(y_ready, 8 * q + m - 1)
                if m in (5, 6):
                    pe.wait_ge(mem_normed, l * 2 + 2)
                    for k in range(4 * (m - 5), 4 * (m - 4)):
                        if k >= 4:
                            pe.wait_ge(m_lo_ready, l * 8 + k - 3)
                        for i in range(2):
                            mm = turn(psum[:, 4 + k % 4, i * 128:(i + 1) * 128], mem[:, i, k * 128:(k + 1) * 128])
                        mm.then_inc(mem_turned, 1)
                chunk(base + AT_OUT + m // 2, m % 2, 2 * (m % 2), u_in, range(KD), True, True).then_inc(chunk_done, 1)
            norm_y(q)

            pe.wait_ge(y_ready, 8 * (q + 1))
            for m in range(KD + 1):
                if m < KD:
                    if m >= 2:
                        pe.wait_ge(kv_kept, l * 8 + m - 1)
                    chunk(base + AT_CKV + m // 2, m % 2, m % 2, lambda k: (m_hi[:, k, :], m_lo[:, k, :]), range(KD),
                          True, True, count=(lambda k: pe.wait_ge(m_lo_ready, l * 8 + k + 1)) if m == 0 else None
                          ).then_inc(chunk_done, 1)
                if m == 0:
                    spread_r(q)
                if m >= 1:
                    t = m - 1
                    pe.wait_ge(kv_kept, l * 8 + t + 1)
                    if t >= 2:
                        pe.wait_ge(kv_nat, l * 8 + t - 1)
                    src = mk_t[:, t, :] if t < 4 else mv_t[:, t % 2, :]
                    for i in range(2):
                        mm = turn(psum[:, 2 + t % 2, i * 128:(i + 1) * 128], src[:, i * 128:(i + 1) * 128])
                    mm.then_inc(kv_turned, 1)

            q = 4 * l + 2
            pe.wait_ge(kv_nat, l * 8 + 8)
            first_chunks(base + AT_CQ, q)
            pe.wait_ge(r_kept, q)
            norm_x(q, 6)
            for m in range(2, 4):
                if m == 3:
                    pe.wait_ge(qc_ready, l * 4 + 2)
                chunk(base + AT_CQ + 1, m % 2, CQ_BANK[m], u_in, range(KD), True, True).then_inc(chunk_done, 1)
            pe.wait_ge(qc_ready, l * 4 + 4)
            attention(l, CROSS)

            pe.wait_ge(split_lo, (l + 1) * TOTAL["split"])
            for j in range(4):
                pe.wait_ge(w_lo_ready, 2 * (base + AT_CO) + j + 1)
                for t in range(2):
                    m = 2 * j + t
                    if m >= 2:
                        pe.wait_ge(y_ready, 8 * q + m - 1)
                    for k in range(4):
                        product(j % 2, 2 * k + t, 2 * t, u_in(k), k == 0, k == 3)
                    if t == 1:
                        pe_last[0].then_inc(chunk_done, 1)
                    else:
                        pe_last[0].then_inc(cross_tile, 1)
            norm_y(q)
            spread_r(q)
            ffn(l, 1)

        pe.wait_ge(x_ready, 8 + 64 * DEPTH // 2)
        for i in range(NT + 1):
            if i >= 2:
                pe.wait_ge(y_kept, i - 1)
            for k in range(KD):
                mm = turn(slot_ap(i % 2, rows_of(i), 128, k * 128), x[:, k, i * 128:i * 128 + rows_of(i)])
            mm.then_inc(y_turned, 1)

    @block.scalar
    def _(act):
        def copy(out, src, scale=1.0):
            return act.activation(out, src, ACT.Copy, scale=scale)

        def cut_hi(pair, slot, first=False, n=8):
            act.wait_ge(w_loaded[slot], 16 * (pair + 1))
            if not first:
                act.wait_ge(chunk_done, 2 * pair + slot - 1)
            copy(w_blocks(w_hi, slot, n), w_blocks(w_raw, slot, n)).then_inc(w_hi_ready, 1)

        def square_of(tile, q, k):
            if not (isinstance(q, int) and k < 2):
                act.wait_ge(summed, 14 * q + k - 1)
            act.activation(square[:, k % 2, :], tile, ACT.Square).then_inc(squared, 1)

        def root_of(bank, index, free):
            act.wait_ge(norm_sum, index + 1)
            act.wait_ge(*free)
            act.activation(two(root[:, :]), banks(bank), ACT.Sqrt, bias=eps[:, :], scale=1.0 / D).then_inc(root_ready, 1)

        def post_root_of(q):
            act.wait_ge(norm_sum, 2 * q + 2)
            act.activation(root_col[:, :], psum[:, 6, 0:NT + 1], ACT.Sqrt, bias=eps[:, :], scale=1.0 / D
                           ).then_inc(root_ready, 1)
            act.wait_ge(r_spread, q + 1)
            act.wait_ge(r_ready, 2 * q + 1)
            copy(root[:, :], flat[:, 3072:3072 + T]).then_inc(r_kept, 1)

        def keep_y(y, q, m, parity):
            act.wait_ge(summed, 14 * q + 7 + m - 1)
            act.activation(two(square[:, parity, :]), banks(2 * parity), ACT.Square).then_inc(squared, 1)
            copy(two(y[:, m, :]), banks(2 * parity)).then_inc(y_ready, 1)

        def next_input(q, gain):
            for k in range(KD):
                next_tile(q, k, gain)

        def next_tile(q, k, gain):
            act.wait_ge(x_ready, 8 * q + k + 1)
            act.activation(u_hi[:, k, :], x[:, k, :], ACT.Copy, scale=gains[:, k, gain:gain + 1]).then_inc(u_hi_ready, 1)
            square_of(x[:, k, :], q, k)

        def warm(function):
            act.activation(warmed[:, :], eps[:, :], function).then_inc(warm_done, 1)

        def ffn(l, f, gain):
            q, n = 4 * l + 3 * f, 2 * l + f
            base = l * PAIRS + AT_FFN[f]

            def tile(pair, parity, local, n_next=8, head=None):
                cut_hi(pair + 1, 0, n=n_next)
                if head:
                    head()
                act.wait_ge(gate_scaled, n * KF + local + 1)
                act.activation(gate[:, parity, :], gate[:, parity, :], ACT.Silu).then_inc(gate_silu, 1)
                cut_hi(pair + 1, 1, n=n_next)
                act.wait_ge(hidden, n * KF + local + 1)
                copy(tile_of(h_hi, local), up[:, parity, :]).then_inc(h_hi_ready, 1)

            tile(base, 0, 0, head=lambda: root_of(6, 2 * q, (x_ready, 8 * q + 8)))
            tile(base + 1, 1, 1)
            with act.Fori(1, GU // 2 - 1) as j:
                for s in range(2):
                    tile(base + 2 * j + s, s, 2 * j + s)
            tile(base + GU - 2, 0, GU - 2)
            tile(base + GU - 1, 1, GU - 1, n_next=DNB)

            def down(m, parity, cut, n_next):
                cut(m, 0, n_next)
                act.wait_ge(chunk_done, 2 * (base + GU + m) + 2)
                keep_y(y_ffn, q, m, parity)
                cut(m, 1, n_next)

            def cut(m, s, n_next):
                cut_hi(base + GU + m + 1, s, n=n_next)
            warm(ACT.Sqrt)
            for m in range(DN - 1):
                down(m, m % 2, cut, DNB)
            down(DN - 1, 1, cut, 8)
            post_root_of(q)
            next_input(q + 1, gain)

        def attention(l, steps):
            for step in steps:
                for it in step["uses"]:
                    if it["use"] != "score":
                        continue
                    u = it["of"]
                    rows, n, s = rows_of(u["i"]), keys_of(u), it["score"]
                    p = probs_at(it)[0:rows, 0:n]
                    if u["kind"] == "C":
                        act.wait_ge(negated, l * 20 + it["unit_here"] + 1)
                        if it["before"]:
                            act.wait_ge(turned, l * TOTAL["unit"] + it["before"]["unit"] + 1)
                        act.activation(p, slot_ap(it["slot"] % 2, rows, n), ACT.Exp, bias=negmax[0:rows, s % 8:s % 8 + 1],
                                       accum_out=rowsum[0:rows, s % 8:s % 8 + 1]).then_inc(expd, 1)
                    else:
                        act.wait_ge(biased, l * TOTAL["biased"] + it["biased"] + 1)
                        act.activation(p, p, ACT.Exp, bias=negmax[0:rows, s % 8:s % 8 + 1], scale=-1.0,
                                       accum_out=rowsum[0:rows, s % 8:s % 8 + 1]).then_inc(expd, 1)
                        if u["kind"] == "B" and u["i"] == 0 and it["map"] == 0 and u["h"] < 3:
                            scale_table(l, u["h"] + 1)
                        if u["kind"] == "A" and u["i"] == 0 and u["h"] == 7:
                            scale_table(l, 0)
                for u in step["turn"]:
                    ub, rows, n = u["unit"] % 2, rows_of(u["i"]), keys_of(u)
                    act.wait_ge(turned, l * TOTAL["unit"] + u["unit"] + 1)
                    if u["unit"] >= 2:
                        act.wait_ge(values_done, l * TOTAL["unit"] + u["unit"] - 1)
                    full = n // 128 * rows
                    copy(probs_t[:, ub, 0:full], psum[:, 4 + ub, 0:full]).then_inc(turned_kept, 1)
                    if n % 128:
                        copy(probs_t[0:n % 128, ub, full:full + rows], psum[0:n % 128, 4 + ub, full:full + rows]
                             ).then_inc(turned_kept, 1)

        def scale_table(l, h):
            act.wait_ge(biased, l * TOTAL["biased"] + (7 * 5 if h == 0 else 40 + 10 * (h - 1)))
            copy(table[:, h % 2, :], dist[:, :], scale=-SLOPES[h]).then_inc(tab_scaled, 1)

        act.dma_start(x_nat[:, 0:NT, :], x_prompt.rearrange("b (i p) d -> p (b i) d", p=128)).then_inc(x_loaded, 16)
        act.dma_start(x_nat[0:SAMPLE, NT, :], x_sample[0]).then_inc(x_loaded, 16)
        for s in range(2):
            cut_hi(0, s, first=True)
        act.wait_ge(dist_ready, 1)
        act.activation(dist[:, :], dist[:, :], ACT.Abs).then_inc(dist_ready, 1)
        act.wait_ge(lam_dots, 2 * DEPTH)
        act.activation(lam_exp[:, :], lam_dot[:, :], ACT.Exp).then_inc(lam_exps, 1)
        act.wait_ge(dist_ready, 3)
        act.wait_ge(layer_gains, 1)
        next_input(0, 8)

        with act.Fori(0, DEPTH) as l:
            base = l * PAIRS
            ffn(l, 0, 2)

            q = 4 * l + 1
            for g in range(2):
                for m in range(12):
                    last = g == 1 and m >= 10
                    cut_hi(base + AT_IN + g * 6 + m // 2 + 1, m % 2)
                    if g == 0 and m == 0:
                        root_of(4, 2 * q, (x_ready, 8 * q + 8))
                    if m < 8:
                        act.wait_ge(fresh_ready, l * 24 + g * 12 + m + 1)
                        copy(qk[:, g * 8 + m, :], fresh[:, m % 2, :], scale=0.125 if m < 4 else 1.0).then_inc(qk_kept, 1)
            warm(ACT.Exp)
            attention(l, OWN)
            act.wait_ge(head_sq, l * 20 + 20)
            act.activation(headroot[:, :], headsq[:, :], ACT.Sqrt, bias=eps[:, :], scale=1.0 / 128).then_inc(head_root, 1)

            for m in range(KD):
                if m == 2:
                    act.wait_ge(mem_loaded, l * 16 + 16)
                    for i in range(2):
                        if i == 1:
                            act.wait_ge(mem_sq, l * 2 + 1)
                        act.activation(memsquare[:, :], mem[:, i, :], ACT.Square, accum_out=memsq[:, i:i + 1]).then_inc(mem_sq, 1)
                    act.wait_ge(mem_sq, l * 2 + 2)
                    act.activation(memroot[:, :], memsq[:, :], ACT.Sqrt, bias=eps[:, :], scale=1.0 / D).then_inc(mem_root, 1)
                if m in (5, 6):
                    for k in range(4 * (m - 5), 4 * (m - 4)):
                        act.wait_ge(mem_turned, l * 8 + k + 1)
                        act.activation(m_hi[:, k, :], psum[:, 4 + k % 4, 0:NMEM], ACT.Copy, scale=gains[:, k, 9:10]).then_inc(m_hi_ready, 1)
                act.wait_ge(chunk_done, 2 * (base + AT_OUT) + m + 1)
                keep_y(y_mix, q, m, m % 2)
                cut_hi(base + AT_OUT + m // 2 + 1, m % 2)
            post_root_of(q)
            for m in range(KD):
                cut_hi(base + AT_CKV + m // 2 + 1, m % 2)
                next_tile(q + 1, m, 4)

            q = 4 * l + 2
            for m in range(4):
                cut_hi(base + AT_CQ + m // 2 + 1, m % 2)
                if m == 0:
                    root_of(6, 2 * q, (x_ready, 8 * q + 8))
            attention(l, CROSS)
            warm(ACT.Sqrt)
            for j in range(4):
                for t in range(2):
                    if t == 0:
                        act.wait_ge(cross_tile, l * 4 + j + 1)
                    else:
                        act.wait_ge(chunk_done, 2 * (base + AT_CO) + j + 1)
                    keep_y(y_mix, q, 2 * j + t, t)
                cut_hi(base + AT_CO + j // 2 + 1, j % 2)
            post_root_of(q)
            next_input(q + 1, 6)
            ffn(l, 1, 8)

        for i in range(NT + 1):
            act.wait_ge(y_kept, i + 1)
            dst = y_prompt[0, i * 128:(i + 1) * 128, :] if i < NT else y_sample[0]
            act.dma_start(dst, y_nat[0:rows_of(i), i % 2, :]).then_inc(y_stored[i % 2], 16)
        act.wait_ge(y_stored[0], 48)
        act.wait_ge(y_stored[1], 32)

    @block.vector
    def _(dve):
        def stt(out, a, scalar, b, op0, op1):
            return dve.scalar_tensor_tensor(out=out, in0=a, scalar=scalar, in1=b, op0=op0, op1=op1)

        def cut_lo(pair, slot, n=8):
            dve.wait_ge(w_hi_ready, 2 * pair + slot + 1)
            dve.tensor_tensor(w_blocks(w_lo, slot, n), w_blocks(w_raw, slot, n),
                              w_blocks(w_hi, slot, n).bitcast(F32), ALU.subtract).then_inc(w_lo_ready, 1)

        def inverse(out, index):
            dve.wait_ge(root_ready, index + 1)
            dve.reciprocal(out, root[:, :]).then_inc(r_ready, 1)
            dve.wait_ge(r_ready, index + 1)

        def next_input(q, gain):
            for k in range(KD):
                low_input(q, k, gain)

        def low_input(q, k, gain):
            dve.wait_ge(u_hi_ready, 8 * q + k + 1)
            stt(u_lo[:, k, :], x[:, k, :], gains[:, k, gain:gain + 1], u_hi[:, k, :].bitcast(F32),
                ALU.mult, ALU.subtract).then_inc(u_lo_ready, 1)

        def sum_y_squares(q, m):
            if m >= 1:
                dve.wait_ge(squared, 16 * q + 8 + m + 1)
                if m > 1:
                    dve.wait_ge(summed, 14 * q + 7 + m - 1)
                dve.tensor_tensor(sumsq[:, :], square[:, 0, :] if m == 1 else sumsq[:, :], square[:, m % 2, :],
                                  ALU.add).then_inc(summed, 1)

        def update(q, y, post, gain, between=None):
            dve.wait_ge(root_ready, 2 * q + 2)
            dve.reciprocal(inv_col[:, :], root_col[:, :]).then_inc(r_ready, 1)
            dve.wait_ge(r_kept, q + 1)
            for k in range(KD):
                dve.tensor_tensor(y[:, k, :], y[:, k, :], root[:, :], ALU.mult).then_inc(y_normed, 1)
                if k:
                    low_input(q + 1, k - 1, gain)
                dve.wait_ge(y_normed, 8 * q + k + 1)
                stt(x[:, k, :], y[:, k, :], gains[:, k, post:post + 1], x[:, k, :], ALU.mult, ALU.add).then_inc(x_ready, 1)
                if between:
                    between(k)
            low_input(q + 1, KD - 1, gain)

        def ffn(l, f, post, gain):
            q, n = 4 * l + 3 * f, 2 * l + f
            base = l * PAIRS + AT_FFN[f]

            def tile(pair, parity, local, n_next=8, head=None):
                if head:
                    cut_lo(pair + 1, 0, n_next)
                    head()
                dve.wait_ge(chunk_done, 2 * pair + 1)
                if not (isinstance(local, int) and local < 2):
                    dve.wait_ge(h_hi_ready, n * KF + local - 1)
                    dve.wait_ge(h_lo_ready, n * KF + local - 1)
                dve.tensor_tensor(two(gate[:, parity, :]), banks(4 * parity), two(r_pre[:, :]), ALU.mult).then_inc(gate_scaled, 1)
                if not head:
                    cut_lo(pair + 1, 0, n_next)
                dve.wait_ge(chunk_done, 2 * pair + 2)
                dve.tensor_tensor(two(up[:, parity, :]), banks(4 * parity + 2), two(r_pre[:, :]), ALU.mult).then_inc(up_scaled, 1)
                dve.wait_ge(gate_silu, n * KF + local + 1)
                dve.wait_ge(up_scaled, n * KF + local + 1)
                dve.tensor_tensor(up[:, parity, :], up[:, parity, :], gate[:, parity, :], ALU.mult).then_inc(hidden, 1)
                cut_lo(pair + 1, 1, n_next)
                dve.wait_ge(h_hi_ready, n * KF + local + 1)
                dve.tensor_tensor(tile_of(h_lo, local), up[:, parity, :], tile_of(h_hi, local).bitcast(F32),
                                  ALU.subtract).then_inc(h_lo_ready, 1)

            tile(base, 0, 0, head=lambda: inverse(r_pre[:, :], 2 * q))
            tile(base + 1, 1, 1)
            with dve.Fori(1, GU // 2 - 1) as j:
                for s in range(2):
                    tile(base + 2 * j + s, s, 2 * j + s)
            tile(base + GU - 2, 0, GU - 2)
            tile(base + GU - 1, 1, GU - 1, n_next=DNB)
            for m in range(DN):
                for s in range(2):
                    if s == 1:
                        sum_y_squares(q, m)
                    cut_lo(base + GU + m + 1, s, DNB if m < DN - 1 else 8)
            update(q, y_ffn, post, gain)

        def attention(l, steps):
            for t, step in enumerate(steps):
                for it in step["uses"]:
                    slot = it["slot"] % 2
                    if it["use"] == "score":
                        bias(l, it, slot)
                    elif it["use"] == "cache":
                        dve.wait_ge(slot_ready, l * TOTAL["slot"] + it["slot"] + 1)
                        into = (cmk_t if it["of_kind"] == "C" else kc_t)[:, :, it["tile"] * 128:(it["tile"] + 1) * 128]
                        dve.tensor_copy(into, slot_ap(slot, 128, 512).rearrange("p (m n) -> p m n", m=4)).then_inc(cache_kept, 1)
                    elif it["tile"] < 4:
                        out_tile(l, it, slot)
                for u in steps[t + 1]["turn"] if t + 1 < len(steps) else []:
                    if u["kind"] == "B":
                        combine(l, u)
                for u in step["value"]:
                    keep_values(l, u)

        def out_tile(l, it, slot):
            tile = it["tile"]
            dve.wait_ge(slot_ready, l * TOTAL["slot"] + it["slot"] + 1)
            src = slot_ap(slot, 128, T)
            if tile >= 4:
                dve.tensor_scalar(u_hi[:, tile, :], src, sub_gain[:, :], None, ALU.mult).then_inc(split_hi, 1)
            else:
                dve.tensor_copy(u_hi[:, tile, :], src).then_inc(split_hi, 1)
            dve.wait_ge(split_hi, l * TOTAL["split"] + it["split"] + 1)
            high = u_hi[:, tile, :].bitcast(F32)
            if tile >= 4:
                stt(u_lo[:, tile, :], src, sub_gain[:, :], high, ALU.mult, ALU.subtract).then_inc(split_lo, 1)
            else:
                dve.tensor_tensor(u_lo[:, tile, :], src, high, ALU.subtract).then_inc(split_lo, 1)

        def bias(l, it, slot):
            u, s = it["of"], it["score"]
            rows, n = rows_of(u["i"]), keys_of(u)
            col = slice(s % 8, s % 8 + 1)
            dve.wait_ge(slot_ready, l * TOTAL["slot"] + it["slot"] + 1)
            if u["kind"] == "C":
                dve.reduce_max(negmax[0:rows, col], slot_ap(slot, rows, n), AX.X).then_inc(rowmax, 1)
                dve.wait_ge(rowmax, l * 20 + it["unit_here"] + 1)
                dve.tensor_scalar(negmax[0:rows, col], negmax[0:rows, col], -1.0, None, ALU.mult).then_inc(negated, 1)
                return
            if u["kind"] == "A":
                head = u["h"]
                dve.wait_ge(tab_loaded[head % 2], l * 64 + 16 * (head // 2 + 1))
            else:
                head = u["h"]
                dve.wait_ge(tab_scaled, l * 4 + head + 1)
            if it["before"]:
                dve.wait_ge(turned, l * TOTAL["unit"] + it["before"]["unit"] + 1)
            settled(dve)
            start = PAST - 128 * u["i"]
            dve.tensor_tensor_reduce(out=probs_at(it)[0:rows, 0:n], in0=slot_ap(slot, rows, n),
                                     in1=table[0:rows, head % 2, start:start + n], scale=-1.0, scalar=3e38,
                                     op0=ALU.add, op1=ALU.min, accum_out=negmax[0:rows, col]).then_inc(biased, 1)

        def combine(l, u):
            s0, s1 = (it["score"] for it in u["scores"])
            first, second = (probs_at(it) for it in u["scores"])
            rows, n = rows_of(u["i"]), keys_of(u)
            c = l * TOTAL["combined"] + u["combined"]
            par = u["combined"] % 2
            dve.wait_ge(expd, l * TOTAL["expd"] + u["scores"][1]["expd"] + 1)
            dve.reciprocal(rowinv[0:rows, s1 % 8:s1 % 8 + 1], rowsum[0:rows, s1 % 8:s1 % 8 + 1]).then_inc(inverted, 1)
            dve.wait_ge(inverted, c + 1)
            stt(mapscale[0:rows, par:par + 1], rowsum[0:rows, s0 % 8:s0 % 8 + 1], neglam[0:rows, :],
                rowinv[0:rows, s1 % 8:s1 % 8 + 1], ALU.mult, ALU.mult).then_inc(mapscaled, 1)
            dve.wait_ge(mapscaled, c + 1)
            stt(first[0:rows, 0:n], second[0:rows, 0:n], mapscale[0:rows, par:par + 1],
                first[0:rows, 0:n], ALU.mult, ALU.add).then_inc(combined, 1)

        def keep_nat(l, g, m):
            index, par = g * 8 + m - 4, m % 2
            if g == 1 and m == 4:
                dve.wait_ge(k_stored, l * 64 + 32)
            dve.wait_ge(fresh_turned, l * 16 + index + 1)
            into = k_nat[:, :, (m - 4) * 128:(m - 3) * 128] if m < 8 else \
                v_nat[:, :, g * 512 + (m - 8) * 128:g * 512 + (m - 7) * 128]
            src = flat[:, 2048 + par * 1024:2048 + par * 1024 + 640].rearrange("p (i n) -> p i n", n=128)
            dve.tensor_copy(into[:, 0:NT, :], src[:, 0:NT, :]).then_inc(nat_kept, 1)
            dve.tensor_copy(into[0:SAMPLE, NT, :], src[0:SAMPLE, NT, :]).then_inc(nat_kept, 1)

        def keep_values(l, u):
            i, h, s = u["i"], u["h"], u["scores"][0]["score"]
            rows = rows_of(i)
            col = slice(s % 8, s % 8 + 1)
            dve.wait_ge(values_done, l * TOTAL["unit"] + u["unit"] + 1)
            dve.reciprocal(rowinv[0:rows, col], rowsum[0:rows, col]).then_inc(rowinverted, 1)
            dve.wait_ge(rowinverted, l * TOTAL["unit"] + u["unit"] + 1)
            if u["kind"] == "A":
                part = slice(64 * (h % 2), 64 * (h % 2) + 64)
                out = o_nat[0:rows, h // 2, i, part]
            else:
                part = slice(0, 128)
                out = o_nat[0:rows, h, i, :]
            dve.tensor_scalar(out, psum[0:rows, 6 + u["unit"] % 2, part], rowinv[0:rows, col], None,
                              ALU.mult).then_inc(o_kept, 1)
            if u["kind"] == "B":
                dve.wait_ge(o_kept, l * TOTAL["unit"] + u["unit"] + 1)
                n = u["combined"]
                if n:
                    dve.wait_ge(head_sq, l * 20 + n)
                dve.tensor_tensor_reduce(out=headsquare[0:rows, :], in0=out, in1=out, scale=1.0, scalar=0.0,
                                         op0=ALU.mult, op1=ALU.add,
                                         accum_out=headsq[0:rows, h * (NT + 1) + i:h * (NT + 1) + i + 1]).then_inc(head_sq, 1)

        for s in range(2):
            cut_lo(0, s)
        dve.memset(headsq[:, :], 1.0).then_inc(setup_done, 1)
        dve.wait_ge(setup_loaded, 80)
        dve.tensor_copy(bias_rev[:, 511:767], bias_in[:, 256:0:-1]).then_inc(rev_ready, 1)
        dve.tensor_copy(bias_rev[:, 0:511], bias_in[:, 256:257].broadcast_to([16, 511])).then_inc(rev_ready, 1)
        for n in range(2 * DEPTH):
            if n:
                dve.wait_ge(lam_dots, n)
            dve.tensor_tensor_reduce(out=lam_prod[:, :], in0=lam_in[:, n // 2, 2 * (n % 2), :],
                                     in1=lam_in[:, n // 2, 2 * (n % 2) + 1, :], scale=1.0, scalar=0.0,
                                     op0=ALU.mult, op1=ALU.add, accum_out=lam_dot[:, n:n + 1]).then_inc(lam_dots, 1)
        dve.wait_ge(dist_ready, 2)
        dve.memset(dist[0:64, 576:640], 1e32).then_inc(dist_ready, 1)
        dve.wait_ge(lam_exps, 1)
        for n in range(DEPTH):
            stt(neglam_all[:, n:n + 1], lam_exp[:, 2 * n + 1:2 * n + 2], LAM_INIT[n],
                lam_exp[:, 2 * n:2 * n + 1], ALU.subtract, ALU.subtract).then_inc(setup_vals, 1)
        dve.wait_ge(setup_t, 1)
        dve.tensor_copy(gains_all[:, :, :], psum[:, 4, 0:KD * 18].rearrange("p (k n) -> p k n", k=KD)).then_inc(setup_vals, 1)
        for n in range(DEPTH):
            dve.tensor_scalar(sub_all[:, n:n + 1], psum[:, 4, KD * 18 + n:KD * 18 + n + 1], 1.0 - LAM_INIT[n], None,
                              ALU.mult).then_inc(setup_vals, 1)
        dve.wait_ge(setup_vals, 5)
        dve.tensor_copy(gains[:, :, 8:9], gains_all[:, :, 0:1]).then_inc(layer_gains, 1)
        dve.wait_ge(layer_gains, 1)
        dve.wait_ge(setup_done, 1)
        for k in range(KD):
            dve.wait_ge(x_turned, k + 1)
            dve.tensor_copy(x[:, k, :], slot_ap(k % 2, 128, T)).then_inc(x_ready, 1)
        for k in range(KD):
            low_input(0, k, 8)

        with dve.Fori(0, DEPTH) as l:
            base = l * PAIRS
            dve.wait_ge(u_lo_ready, 8 + 32 * l)
            dve.tensor_copy(gains[:, :, 0:9], gains_all[:, :, bass.ds(l * 8, 9)]).then_inc(gains_now, 1)
            dve.tensor_copy(gains[:, :, 9:10], gains_all[:, :, bass.ds(l + 16, 1)]).then_inc(gains_now, 1)
            dve.tensor_copy(neglam[:, :], neglam_all[:, bass.ds(l, 1)]).then_inc(gains_now, 1)
            dve.tensor_copy(sub_gain[:, :], sub_all[:, bass.ds(l, 1)]).then_inc(gains_now, 1)
            dve.wait_ge(gains_now, 6 * l + 4)
            for n in (1, 7):
                dve.tensor_scalar(gains[:, :, n:n + 1], gains[:, :, n:n + 1], 0.5, None, ALU.mult).then_inc(gains_now, 1)
            dve.wait_ge(gains_now, 6 * l + 6)
            ffn(l, 0, 1, 2)

            q = 4 * l + 1
            for g in range(2):
                for m in range(12):
                    w = g * 12 + m
                    if w == 0:
                        cut_lo(base + AT_IN + 1, 0)
                        inverse(r_pre[:, :], 2 * q)
                    dve.wait_ge(chunk_done, 2 * (base + AT_IN) + w + 1)
                    if w >= 2:
                        before = w - 2
                        bg, bm = divmod(before, 12)
                        if bm < 8:
                            dve.wait_ge(qk_kept, l * 16 + bg * 8 + bm + 1)
                        if bm >= 4:
                            dve.wait_ge(fresh_turned, l * 16 + bg * 8 + bm - 4 + 1)
                    dve.tensor_tensor(two(fresh[:, m % 2, :]), banks(in_bank(g, m)), two(r_pre[:, :]), ALU.mult).then_inc(fresh_ready, 1)
                    if w:
                        cut_lo(base + AT_IN + w // 2 + 1, w % 2)
                    if m >= 5:
                        keep_nat(l, g, m - 1)
                keep_nat(l, g, 11)
            dve.wait_ge(k_stored, l * 64 + 64)
            attention(l, OWN)
            dve.wait_ge(head_root, l + 1)
            dve.reciprocal(headinv[:, :], headroot[:, :]).then_inc(head_inv, 1)
            dve.wait_ge(head_inv, l + 1)
            for h in range(4):
                inv = headinv[:, h * (NT + 1):(h + 1) * (NT + 1)].rearrange("p (i o) -> p i o", o=1)
                o = o_nat[:, h, 0:NT, :]
                dve.tensor_tensor(o, o, inv[:, 0:NT, :].broadcast_to([128, NT, 128]), ALU.mult).then_inc(head_normed, 1)
                o = o_nat[0:SAMPLE, h, NT, :]
                dve.tensor_scalar(o, o, headinv[0:SAMPLE, h * (NT + 1) + NT:(h + 1) * (NT + 1)], None, ALU.mult).then_inc(head_normed, 1)
            for it in OWN[-1]["uses"]:
                out_tile(l, it, it["slot"] % 2)

            for m in range(KD):
                if m in (5, 6):
                    for k in range(4 * (m - 5), 4 * (m - 4)):
                        dve.wait_ge(m_hi_ready, l * 8 + k + 1)
                        stt(m_lo[:, k, :], psum[:, 4 + k % 4, 0:NMEM], gains[:, k, 9:10], m_hi[:, k, :].bitcast(F32),
                            ALU.mult, ALU.subtract).then_inc(m_lo_ready, 1)
                sum_y_squares(q, m)
                cut_lo(base + AT_OUT + m // 2 + 1, m % 2)
                if m == 2:
                    dve.wait_ge(mem_root, l + 1)
                    dve.reciprocal(meminv[:, :], memroot[:, :]).then_inc(mem_inv, 1)
                    dve.wait_ge(mem_inv, l + 1)
                    for i in range(2):
                        dve.tensor_scalar(mem[:, i, :], mem[:, i, :], meminv[:, i:i + 1], None, ALU.mult).then_inc(mem_normed, 1)

            def memory_tile(m):
                if m < KD:
                    dve.wait_ge(chunk_done, 2 * (base + AT_CKV) + m + 1)
                    if m >= 6:
                        dve.wait_ge(kv_turned, l * 8 + m - 1)
                    dst = mk_t[:, m, :] if m < 4 else mv_t[:, m % 2, :]
                    dve.tensor_copy(dst, psum[:, m % 2, 0:NMEM]).then_inc(kv_kept, 1)
                    cut_lo(base + AT_CKV + m // 2 + 1, m % 2)
                if m >= 1:
                    t = m - 1
                    dve.wait_ge(kv_turned, l * 8 + t + 1)
                    dst = (mk_nat if t < 4 else mv_nat)[:, :, (t % 4) * 128:(t % 4 + 1) * 128]
                    dve.tensor_copy(dst, psum[:, 2 + t % 2, 0:NMEM].rearrange("p (i n) -> p i n", i=2)).then_inc(kv_nat, 1)
            update(q, y_mix, 3, 4, memory_tile)
            memory_tile(KD)

            q = 4 * l + 2
            for m in range(4):
                cut_lo(base + AT_CQ + m // 2 + 1, m % 2)
                if m == 0:
                    inverse(r_pre[:, :], 2 * q)
                dve.wait_ge(chunk_done, 2 * (base + AT_CQ) + m + 1)
                stt(two(qc[:, m, :]), banks(CQ_BANK[m]), 128 ** -0.5, two(r_pre[:, :]), ALU.mult, ALU.mult).then_inc(qc_ready, 1)
            attention(l, CROSS)
            for j in range(4):
                sum_y_squares(q, 2 * j)
                sum_y_squares(q, 2 * j + 1)
                cut_lo(base + AT_CO + j // 2 + 1, j % 2)
            update(q, y_mix, 5, 6)
            dve.wait_ge(mem_stored, l * 32 + 32)
            ffn(l, 1, 7, 8)

        for i in range(NT + 1):
            dve.wait_ge(y_turned, i + 1)
            if i >= 2:
                dve.wait_ge(y_stored[i % 2], 16 * (i // 2))
            dve.tensor_copy(y_nat[0:rows_of(i), i % 2, :], slot_ap(i % 2, rows_of(i), D)).then_inc(y_kept, 1)

    block_cm.__exit__(None, None, None)


_INS = ["x_prompt", "x_sample", "mem_prompt", "cache_a_k", "cache_a_v", "cache_b_k", "cache_b_v",
        "cache_mem_k", "cache_mem_v", "norm_g", "w_ffn_gu", "w_ffn_dn", "w_in", "rel_bias",
        "diff_lambda", "subln_g", "w_out", "mem_norm_g", "w_cq", "w_ckv", "w_co"]
_OUTS = [(1, SEQ, D), (1, SAMPLE, D), (DEPTH, 1, SEQ, 8, 64), (DEPTH, 1, SEQ, 8, 64),
         (DEPTH, 1, SEQ, 4, 2, 64), (DEPTH, 1, SEQ, 4, 128), (DEPTH, 1, NMEM, 4, 128), (DEPTH, 1, NMEM, 4, 128),
         (DEPTH, 1, SAMPLE, 8, 64), (DEPTH, 1, SAMPLE, 8, 64), (DEPTH, 1, SAMPLE, 4, 2, 64), (DEPTH, 1, SAMPLE, 4, 128)]


def kernel(**inputs):
    import numpy as _np
    import concourse.bacc as _bacc
    from concourse import mybir as _mybir
    from concourse.bass_utils import run_bass_kernel_spmd as _run

    nc = _bacc.Bacc("TRN2", target_bir_lowering=False, num_devices=1)
    arrays, args = {}, []
    for name in _INS:
        a = _np.ascontiguousarray(inputs[name])
        arrays[f"in_{name}"] = a
        args.append(nc.dram_tensor(f"in_{name}", a.shape, _mybir.dt.from_np(a.dtype), kind="ExternalInput").ap())
    for i, shape in enumerate(_OUTS):
        args.append(nc.dram_tensor(f"out_{i}", shape, _mybir.dt.float32, kind="ExternalOutput").ap())
    build(nc, *args)
    r = _run(nc, [arrays], core_ids=[0])
    return tuple(r.results[0][f"out_{i}"] for i in range(len(_OUTS)))
```
